# Optimizing a Trainium2 kernel written in Bass

```python
import math
import jax, jax.numpy as jnp
from jax import lax
import numpy as np

D_MODEL = 2048
BATCH = 1
SEQ = 512
DEPTH = 1

CHUNK = 64
Q_BLOCK = 128
EPS = 1e-6

ATT_HEADS = 8
ATT_KV_HEADS = 2
HEAD_DIM = 128
ATT_WIDTH = ATT_HEADS * HEAD_DIM
KV_WIDTH = ATT_KV_HEADS * HEAD_DIM
IDX_HEADS = 16
IDX_DIM = 64
INDEX_TOPK = 256
ROPE_THETA = 500000.0
ROPE_FRACTION = 4

SSM_GROUP_CH = 16
SSM_GROUPS = 32
SSM_WIDTH = SSM_GROUPS * SSM_GROUP_CH
SSM_STATE = 64
DT_MIN = 0.001
DT_MAX = 0.1

N_BRANCH = 2
SPLITS = (ATT_WIDTH, KV_WIDTH, KV_WIDTH, ATT_WIDTH,
          IDX_HEADS * IDX_DIM, IDX_DIM, IDX_HEADS,
          SSM_WIDTH, SSM_WIDTH,
          N_BRANCH * D_MODEL)
IN_WIDTH = sum(SPLITS)

kernel_name = "hybrid_dsa_s5_gated_merge"

def rms_norm(x, g):
    xf = x.astype(jnp.float32)
    y = xf * lax.rsqrt(jnp.mean(xf * xf, axis=-1, keepdims=True) + EPS)
    return (y * g.astype(jnp.float32)).astype(x.dtype)

def partial_rotary(x, positions):
    rd = x.shape[-1] // ROPE_FRACTION
    half = rd // 2
    inv_freq = jnp.exp(-math.log(ROPE_THETA) * jnp.arange(half, dtype=jnp.float32) * (2.0 / rd))
    ang = positions.astype(jnp.float32)[..., None] * inv_freq
    cos = jnp.cos(ang)[:, :, None, :]
    sin = jnp.sin(ang)[:, :, None, :]
    xf = x.astype(jnp.float32)
    x1, x2 = xf[..., :half], xf[..., half:rd]
    rot = jnp.concatenate([x1 * cos - x2 * sin, x2 * cos + x1 * sin], axis=-1).astype(x.dtype)
    return jnp.concatenate([rot, x[..., rd:]], axis=-1)

def dsa_attention(q, k, v, q_idx, k_idx, w_idx):
    b, l = q.shape[:2]
    n_blk = l // Q_BLOCK
    topk = min(INDEX_TOPK, l // 4)
    grp = ATT_HEADS // ATT_KV_HEADS
    key_chunk = jnp.arange(l) // CHUNK

    def to_blocks(a):
        a = a.reshape((b, n_blk, Q_BLOCK) + a.shape[2:])
        return jnp.moveaxis(a, 1, 0)

    q_blocks = to_blocks(q.reshape(b, l, ATT_KV_HEADS, grp, HEAD_DIM))
    qi_blocks = to_blocks(q_idx)
    w_blocks = to_blocks(w_idx)
    gather = jax.vmap(lambda src, ids: src[ids])

    def one_block(args):
        q_blk, qi_blk, w_blk, blk = args
        q_chunk = (blk * Q_BLOCK + jnp.arange(Q_BLOCK)) // CHUNK
        admissible = key_chunk[None, :] <= q_chunk[:, None]
        logits = jnp.einsum("bqhd,bsd->bqhs", qi_blk, k_idx) * (IDX_DIM ** -0.5)
        score = jnp.einsum("bqhs,bqh->bqs", jax.nn.relu(logits), w_blk).astype(jnp.float32)
        score = jnp.where(admissible[None], score, -jnp.inf)
        _, sel = lax.top_k(score, topk)
        valid = (sel // CHUNK) <= q_chunk[None, :, None]
        k_sel = gather(k, sel)
        v_sel = gather(v, sel)
        s = jnp.einsum("bqhgd,bqkhd->bqhgk", q_blk, k_sel).astype(jnp.float32) * (HEAD_DIM ** -0.5)
        s = jnp.where(valid[:, :, None, None, :], s, -jnp.inf)
        p = jax.nn.softmax(s, axis=-1).astype(v.dtype)
        return jnp.einsum("bqhgk,bqkhd->bqhgd", p, v_sel)

    out = lax.map(one_block, (q_blocks, qi_blocks, w_blocks, jnp.arange(n_blk)))
    return jnp.moveaxis(out, 0, 1).reshape(b, l, ATT_WIDTH)

def s5_combine(e1, e2):
    a1r, a1i, b1r, b1i = e1
    a2r, a2i, b2r, b2i = e2
    return (a2r * a1r - a2i * a1i,
            a2r * a1i + a2i * a1r,
            a2r * b1r - a2i * b1i + b2r,
            a2r * b1i + a2i * b1r + b2i)

def s5_ssm(u, a_re, a_im, log_dt, b_re, b_im, c_re, c_im, d_skip):
    bsz, l = u.shape[:2]
    ug = u.reshape(bsz, l, SSM_GROUPS, SSM_GROUP_CH).astype(jnp.float32)
    dt = jnp.exp(log_dt.astype(jnp.float32))[:, None]
    ar = a_re.astype(jnp.float32)
    ai = a_im.astype(jnp.float32)
    mag = jnp.exp(ar * dt)
    lb_re = mag * jnp.cos(ai * dt)
    lb_im = mag * jnp.sin(ai * dt)
    den = ar * ar + ai * ai
    coef_re = ((lb_re - 1.0) * ar + lb_im * ai) / den
    coef_im = (lb_im * ar - (lb_re - 1.0) * ai) / den
    br = b_re.astype(jnp.float32)
    bi = b_im.astype(jnp.float32)
    bb_re = coef_re[..., None] * br - coef_im[..., None] * bi
    bb_im = coef_re[..., None] * bi + coef_im[..., None] * br
    bu_re = jnp.einsum("blgc,gpc->blgp", ug, bb_re)
    bu_im = jnp.einsum("blgc,gpc->blgp", ug, bb_im)
    a_full_re = jnp.broadcast_to(lb_re, bu_re.shape)
    a_full_im = jnp.broadcast_to(lb_im, bu_im.shape)
    _, _, x_re, x_im = lax.associative_scan(s5_combine, (a_full_re, a_full_im, bu_re, bu_im), axis=1)
    y = (jnp.einsum("blgp,gcp->blgc", x_re, c_re.astype(jnp.float32))
         - jnp.einsum("blgp,gcp->blgc", x_im, c_im.astype(jnp.float32))
         + d_skip.astype(jnp.float32) * ug)
    return y.reshape(bsz, l, SSM_WIDTH).astype(u.dtype)

def hybrid_layer(x, positions, g_norm, w_in, b_merge, a_re, a_im, log_dt, ssm_b_re, ssm_b_im,
                 ssm_c_re, ssm_c_im, ssm_d, w_glu, b_glu, w_att_out, w_ssm_out, w_out):
    bsz, l, _ = x.shape
    h = rms_norm(x, g_norm)
    proj = h @ w_in
    offsets = np.cumsum(SPLITS)[:-1].tolist()
    q, k, v, att_gate, q_idx, k_idx, w_idx, u, ssm_gate, merge = jnp.split(proj, offsets, axis=-1)

    q = partial_rotary(q.reshape(bsz, l, ATT_HEADS, HEAD_DIM), positions)
    k = partial_rotary(k.reshape(bsz, l, ATT_KV_HEADS, HEAD_DIM), positions)
    v = v.reshape(bsz, l, ATT_KV_HEADS, HEAD_DIM)
    q_idx = partial_rotary(q_idx.reshape(bsz, l, IDX_HEADS, IDX_DIM), positions)
    k_idx = partial_rotary(k_idx.reshape(bsz, l, 1, IDX_DIM), positions)[:, :, 0]
    w_idx = w_idx * (IDX_HEADS ** -0.5)
    att = dsa_attention(q, k, v, q_idx, k_idx, w_idx)
    y_a = (att * jax.nn.silu(att_gate)) @ w_att_out

    s = jax.nn.gelu(s5_ssm(u, a_re, a_im, log_dt, ssm_b_re, ssm_b_im, ssm_c_re, ssm_c_im, ssm_d))
    s = s * jax.nn.sigmoid(s @ w_glu + b_glu)
    y_b = (s * jax.nn.silu(ssm_gate)) @ w_ssm_out

    gates = jax.nn.sigmoid(merge + b_merge).reshape(bsz, l, N_BRANCH, D_MODEL)
    mixed = gates[:, :, 0] * y_a + gates[:, :, 1] * y_b
    return x + mixed @ w_out

def setup_inputs(seed: int = 0) -> dict:
    key = jax.random.key(seed)
    ks = jax.random.split(key, 20)
    f32 = jnp.float32

    def nrm(k, shape, scale):
        return jax.random.normal(k, shape, f32) * scale

    x = jax.random.normal(ks[0], (BATCH, SEQ, D_MODEL), f32)
    offset = jax.random.randint(ks[1], (BATCH, 1), 0, 4096, dtype=jnp.int32)
    positions = offset + jnp.arange(SEQ, dtype=jnp.int32)[None, :]
    g_norm = 1.0 + nrm(ks[2], (DEPTH, D_MODEL), 0.01)
    w_in = nrm(ks[3], (DEPTH, D_MODEL, IN_WIDTH), D_MODEL ** -0.5)
    b_merge = nrm(ks[4], (DEPTH, N_BRANCH * D_MODEL), 0.01)
    a_re = -0.5 + nrm(ks[5], (DEPTH, SSM_GROUPS, SSM_STATE), 0.01)
    a_im = (math.pi * jnp.arange(SSM_STATE, dtype=f32))[None, None, :] + nrm(ks[6], (DEPTH, SSM_GROUPS, SSM_STATE), 0.01)
    log_dt = jax.random.uniform(ks[7], (DEPTH, SSM_GROUPS), f32, math.log(DT_MIN), math.log(DT_MAX))
    ssm_b_re = nrm(ks[8], (DEPTH, SSM_GROUPS, SSM_STATE, SSM_GROUP_CH), (2 * SSM_GROUP_CH) ** -0.5)
    ssm_b_im = nrm(ks[9], (DEPTH, SSM_GROUPS, SSM_STATE, SSM_GROUP_CH), (2 * SSM_GROUP_CH) ** -0.5)
    ssm_c_re = nrm(ks[10], (DEPTH, SSM_GROUPS, SSM_GROUP_CH, SSM_STATE), SSM_STATE ** -0.5)
    ssm_c_im = nrm(ks[11], (DEPTH, SSM_GROUPS, SSM_GROUP_CH, SSM_STATE), SSM_STATE ** -0.5)
    ssm_d = nrm(ks[12], (DEPTH, SSM_GROUPS, SSM_GROUP_CH), 1.0)
    w_glu = nrm(ks[13], (DEPTH, SSM_WIDTH, SSM_WIDTH), SSM_WIDTH ** -0.5)
    b_glu = nrm(ks[14], (DEPTH, SSM_WIDTH), 0.01)
    w_att_out = nrm(ks[15], (DEPTH, ATT_WIDTH, D_MODEL), ATT_WIDTH ** -0.5)
    w_ssm_out = nrm(ks[16], (DEPTH, SSM_WIDTH, D_MODEL), SSM_WIDTH ** -0.5)
    w_out = nrm(ks[17], (DEPTH, D_MODEL, D_MODEL), D_MODEL ** -0.5)
    g_final = 1.0 + nrm(ks[18], (D_MODEL,), 0.01)
    return {"x": x, "positions": positions, "g_norm": g_norm, "w_in": w_in, "b_merge": b_merge,
            "a_re": a_re, "a_im": a_im, "log_dt": log_dt, "ssm_b_re": ssm_b_re, "ssm_b_im": ssm_b_im,
            "ssm_c_re": ssm_c_re, "ssm_c_im": ssm_c_im, "ssm_d": ssm_d, "w_glu": w_glu, "b_glu": b_glu,
            "w_att_out": w_att_out, "w_ssm_out": w_ssm_out, "w_out": w_out, "g_final": g_final}

def reference(x, positions, g_norm, w_in, b_merge, a_re, a_im, log_dt, ssm_b_re, ssm_b_im,
              ssm_c_re, ssm_c_im, ssm_d, w_glu, b_glu, w_att_out, w_ssm_out, w_out, g_final):
    for i in range(DEPTH):
        x = hybrid_layer(x, positions, g_norm[i], w_in[i], b_merge[i], a_re[i], a_im[i], log_dt[i],
                         ssm_b_re[i], ssm_b_im[i], ssm_c_re[i], ssm_c_im[i], ssm_d[i], w_glu[i], b_glu[i],
                         w_att_out[i], w_ssm_out[i], w_out[i])
    return rms_norm(x, g_final)


_drawn_inputs = setup_inputs


def setup_inputs(seed=0):
    import zlib

    import numpy as np

    out = dict(_drawn_inputs(seed))
    spreads = {}
    factors = {'g_norm': 8.0,
     'b_merge': 42.529,
     'a_re': 64.0,
     'a_im': 48.168,
     'log_dt': 49.48,
     'ssm_b_re': 64.0,
     'ssm_b_im': 64.0,
     'ssm_c_re': 64.0,
     'ssm_c_im': 64.0,
     'b_glu': 64.0,
     'g_final': 32.297}
    for name, (base, spread) in spreads.items():
        noise = np.random.default_rng([zlib.crc32(name.encode()), seed]).standard_normal(out[name].shape)
        drawn = base * np.exp(spread * noise) if base else spread * noise
        out[name] = __import__('jax').numpy.asarray(drawn.astype(out[name].dtype))
    for name, factor in factors.items():
        out[name] = (out[name] * factor).astype(out[name].dtype)
    return out
```

```python
from contextlib import ExitStack

import concourse.bass as bass
import numpy as np
from concourse import mybir

F32 = mybir.dt.float32
F32R = mybir.dt.float32r
I32 = mybir.dt.int32
ALU = mybir.AluOpType
ACT = mybir.ActivationFunctionType
AX_X = mybir.AxisListType.X

P = 128
SEQ = 512
D = 2048
TOK = SEQ // P
KD = D // P
EPS = 1e-6

HEADS, KV_HEADS, HD = 8, 2, 128
ATT_W, KV_W = HEADS * HD, KV_HEADS * HD
IDX_HEADS, IDX_DIM, TOPK, CHUNK = 16, 64, 128, 64
THETA = 500000.0
GROUPS, GCH, STATE = 32, 16, 64
SSM_W = GROUPS * GCH
PAIRS = GROUPS // 2
QUADS = PAIRS // 4

WIDTHS = (ATT_W, KV_W, KV_W, ATT_W, IDX_HEADS * IDX_DIM, IDX_DIM, IDX_HEADS, SSM_W, SSM_W, 2 * D)
COL_Q, COL_K, COL_V, COL_AG, COL_QI, COL_KI, COL_WI, COL_U, COL_SG, COL_MERGE = (
    int(c) for c in np.cumsum((0,) + WIDTHS[:-1]))

UNIT = 2048
REPLACED = -3.4e38
MASKED = -3.0e38
TOOK_BELOW = -3.2e38
ROUND = 1.5 * 2.0 ** 23
PI = float(np.pi)
INV_2PI = float(1.0 / (2.0 * np.pi))
E_BASE = 32

SEGMENTS = [("kidx", 1, 1), ("qidx", 8, 1), ("k", 2, 1), ("v", 2, 1), ("u", 4, 1), ("q", 8, 1),
            ("attgate", 8, 1), ("attout", 8, 2), ("merge0", 16, 1), ("ssmgate", 4, 1), ("glu", 1, 4),
            ("ssmout", 4, 4), ("merge1", 16, 1), ("out", 16, 1)]
UNIT0, TILE0 = {}, {}
_u = _t = 0
for _name, _n, _k in SEGMENTS:
    UNIT0[_name], TILE0[_name] = _u, _t
    _u, _t = _u + _n, _t + _n * _k
UNITS_END, TILES_END = _u, _t


def split12(x):
    parts = []
    for _ in range(3):
        m, e = np.frexp(x)
        part = float(np.ldexp(np.round(m * 4096.0), e - 12))
        parts.append(part)
        x = x - part
    return parts


def constants():
    row = np.arange(P)
    freq = np.zeros((P, 6), np.float32)
    half = HD // 8
    inv = np.exp(np.float32(-np.log(THETA)) * np.arange(half, dtype=np.float32) * np.float32(2.0 / (2 * half)))
    freq[:, 0] = np.where(row < 2 * half, inv[row % half], 0)
    freq[:, 1] = np.where(row < half, -1, np.where(row < 2 * half, 1, 0))
    half = IDX_DIM // 8
    inv = np.exp(np.float32(-np.log(THETA)) * np.arange(half, dtype=np.float32) * np.float32(2.0 / (2 * half)))
    r = row % IDX_DIM
    freq[:, 2] = np.where(r < 2 * half, inv[r % half], 0)
    freq[:, 3] = np.where(r < half, -1, np.where(r < 2 * half, 1, 0))
    freq[:, 4] = row < STATE
    freq[:, 5] = row >= STATE
    parity = (row[:, None] // GCH) % 2 == (row[None, :] // STATE)
    return {"c_cols": freq, "c_ident": np.eye(P, dtype=np.float32), "c_parity": parity.astype(np.float32)}


def hybrid_kernel(nc, x, positions, g_norm, w_in, b_merge, a_re, a_im, log_dt, b_re, b_im, c_re, c_im, d_skip,
                  w_glu, b_glu, w_att_out, w_ssm_out, w_out, g_final, c_cols, c_ident, c_parity, out):
    w_in_v = w_in[0].rearrange("(k p) n -> p k n", p=P)
    w_att_v = w_att_out[0].rearrange("(k p) n -> p k n", p=P)
    w_ssm_v = w_ssm_out[0].rearrange("(k p) n -> p k n", p=P)
    w_glu_v = w_glu[0].rearrange("(k p) n -> p k n", p=P)
    w_out_v = w_out[0].rearrange("(k p) n -> p k n", p=P)
    x_v = x[0].rearrange("(t p) d -> t p d", p=P)
    out_v = out[0].rearrange("(t p) d -> t p d", p=P)

    with ExitStack() as ctx:
        base = -(-nc.sbuf_base // 64) * 64
        cursor = [base]

        def region(size):
            at = cursor[0]
            cursor[0] += size
            return at

        def at(name, offset, shape, dt=F32):
            return nc.alloc_sbuf_tensor_at(name, [P] + shape, dt, offset=offset)

        KB = 1024
        act_hi = at("act_hi", region(32 * KB), [KD, SEQ], F32R)
        act_lo = at("act_lo", region(32 * KB), [KD, SEQ], F32R)
        w_raw = at("w_raw", region(16 * KB), [2, UNIT])
        w_hi = at("w_hi", region(16 * KB), [2, UNIT], F32R)
        w_lo = at("w_lo", region(16 * KB), [2, UNIT], F32R)
        uT = at("uT", region(8 * KB), [QUADS, SEQ])
        ident = at("ident", region(KB // 2), [P])
        cols = at("cols", region(32), [6])
        g_cols = at("g_cols", region(KB // 2), [96])
        small = at("small", region(KB), [256])

        r1 = region(32 * KB)
        o = [r1]

        def take(name, shape, dt=F32):
            size = int(np.prod(shape)) * 4
            here = o[0]
            o[0] += size
            return at(name, here, shape, dt)

        rot_idx = take("rot_idx", [2, SEQ])
        rot_head = take("rot_head", [2, SEQ])
        kidxT = take("kidxT", [SEQ])
        kT = take("kT", [KV_HEADS, SEQ])
        w_idxT = at("w_idxT", o[0], [SEQ])
        v_tok = take("v_tok", [TOK, KV_W])
        tmp = take("tmp", [2, SEQ])
        w_idx = take("w_idx", [TOK, IDX_HEADS])
        relu = at("relu", o[0], [2, SEQ])
        pT = take("pT", [2, SEQ])
        vT = take("vT", [KV_HEADS, SEQ])
        pos_i = at("pos_i", o[0] - 4 * KB, [SEQ], I32)
        pos_f = at("pos_f", o[0] - 2 * KB, [SEQ])
        assert o[0] <= r1 + 32 * KB
        ya = at("ya", r1, [KD, SEQ])

        r2 = region(32 * KB)
        xt = at("xt", r2, [TOK, D])
        qidxT = at("qidxT", r2, [8, SEQ - P])
        qT = at("qT", r2, [HEADS, SEQ])
        gate_a = at("gate_a", r2 + 16 * KB, [HEADS, SEQ])
        a_hi = at("a_hi", r2, [HEADS, SEQ], F32R)
        o[0] = r2 + 16 * KB
        b_raw = take("b_raw", [2, PAIRS, GCH])
        b_bar = at("b_bar", o[0], [2, PAIRS, GCH])
        b_w = take("b_w", [2, QUADS, P])
        b_blk = take("b_blk", [2, QUADS, 4, 2, GCH])
        e_base = at("e_base", o[0], [2, PAIRS, E_BASE])
        c_nat = take("c_nat", [2, QUADS, P])
        parity = take("parity", [P])
        par = take("par", [21, PAIRS])
        assert o[0] <= r2 + 32 * KB
        o[0] = r2
        e_tab = take("e_tab", [2, SEQ])
        z_ri = take("z_ri", [2, SEQ])
        x_ri = take("x_ri", [2, SEQ])
        prod = take("prod", [2, SEQ])
        assert o[0] <= r2 + 16 * KB
        gate_s = at("gate_s", r2, [QUADS, SEQ])
        gate_glu = at("gate_glu", r2 + 8 * KB, [QUADS, SEQ])
        yb = at("yb", r2, [KD, SEQ])
        res = at("res", r2, [TOK, D])

        r3 = region(16 * KB)
        g_row = at("g_row", r3, [D])
        square = at("square", r3 + 8 * KB, [D])
        o[0] = r3
        score = take("score", [P * 9])
        bias0 = take("bias0", [P])
        probs = take("probs", [3, SEQ])
        assert o[0] <= r3 + 16 * KB
        a_lo = at("a_lo", r3, [HEADS, SEQ], F32R)
        s_hi = at("s_hi", r3, [QUADS, SEQ], F32R)
        s_lo = at("s_lo", r3 + 8 * KB, [QUADS, SEQ], F32R)
        o[0] = r3
        c_w = take("c_w", [2, QUADS, P])
        rot = take("rot", [2, 9, PAIRS])
        r4 = region(4 * KB)
        gate = at("gate", r4, [2, SEQ])
        ang = at("ang", r4, [2, SEQ])
        assert cursor[0] <= nc.sbuf_usable_end, cursor[0]
        nc.alloc_sbuf_tensor("arena", [P, (cursor[0] - nc.sbuf_base) // 4], F32)

        banks = [ctx.enter_context(nc.psum_tensor(f"bank{i}", [P, 512], F32)) for i in range(8)]
        stream_bank, pair_bank, turn_bank, sum_bank = banks[0:2], banks[2:4], banks[4:6], banks[6:8]

        def sem(name):
            return ctx.enter_context(nc.semaphore(name))

        raw_loaded = [sem("raw_loaded0"), sem("raw_loaded1")]
        high_done, split_done = sem("high_done"), sem("split_done")
        slot_claimed = sem("slot_claimed")
        tile_done, tile_free = sem("tile_done"), sem("tile_free")
        x_loaded = [sem(f"x_loaded{t}") for t in range(TOK)]
        consts_loaded, g_loaded, ssm_loaded = sem("consts_loaded"), sem("g_loaded"), sem("ssm_loaded")
        rms_done, h_ready, h_turned, h_high, h_low = (sem(n) for n in ("rms_done", "h_ready", "h_turned", "h_high", "h_low"))
        v_step, a_step = sem("v_step"), sem("a_step")
        ang_ready, table_done = sem("ang_ready"), sem("table_done")
        kidx_ready, kidx_copied = sem("kidx_ready"), sem("kidx_copied")
        qidx_ready, logit_done, relu_done, acc_done = (sem(n) for n in ("qidx_ready", "logit_done", "relu_done", "acc_done"))
        wv_turned, wv_ready = sem("wv_turned"), sem("wv_ready")
        qk_ready = sem("qk_ready")
        scores_done, masked, exp_done, probs_ready, p_turned, pT_ready, pv_done, att_ready = (
            sem(n) for n in ("scores_done", "masked", "exp_done", "probs_ready", "p_turned", "pT_ready", "pv_done", "att_ready"))
        a_high, a_low = sem("a_high"), sem("a_low")
        par_go, par_done = sem("par_go"), sem("par_done")
        ssm_w_ready, ssm_w_turned, c_w_done = sem("ssm_w_ready"), sem("ssm_w_turned"), sem("c_w_done")
        bu_done, bu_used, x_ready, y_done, y_ready, gelu_done = (
            sem(n) for n in ("bu_done", "bu_used", "x_ready", "y_done", "y_ready", "gelu_done"))
        gate_ready, gate_used = sem("gate_ready"), sem("gate_used")
        s_ready, g_ready, m_high, m_low = sem("s_ready"), sem("g_ready"), sem("m_high"), sem("m_low")
        bank_taken, squares_done, final_done, stored = (sem(n) for n in ("bank_taken", "squares_done", "final_done", "stored"))
        res_loaded, gf_loaded, bank_done = sem("res_loaded"), sem("gf_loaded"), sem("bank_done")
        kidx_raw, nmax_ready, bc_loaded, b_w_done, par_loaded = (
            sem(n) for n in ("kidx_raw", "nmax_ready", "bc_loaded", "b_w_done", "par_loaded"))

        block = ctx.enter_context(nc.Block())

        def tiles_through(u):
            for name, n, k in reversed(SEGMENTS):
                if u >= UNIT0[name]:
                    return TILE0[name] + (u - UNIT0[name] + 1) * k
            return 0

        def unit_loop(eng, name, body):
            n = dict((s, c) for s, c, _ in SEGMENTS)[name]
            u0 = UNIT0[name]
            if n < 4:
                for i in range(n):
                    body(u0 + i, (u0 + i) % 2, i)
                return
            with eng.Fori(0, n // 2) as i:
                for half in range(2):
                    body(u0 + half + 2 * i, (u0 + half) % 2, 2 * i + half)

        @block.sync
        def _(sp):
            def raw(slot, k):
                return w_raw[:, slot, :].rearrange("p (k n) -> p k n", k=k)

            def loads(name, source, k):
                def body(u, slot, i):
                    sp.wait_ge(split_done, u - 1)
                    sp.dma_start(raw(slot, k), source(i)).then_inc(raw_loaded[slot], 16)
                unit_loop(sp, name, body)

            def w_in_cols(col):
                return lambda i: w_in_v[:, :, bass.ds(col + P * i, P)]

            sp.dma_start(xt[:, 0, :], x_v[0]).then_inc(x_loaded[0], 16)
            for dst, src in ((cols[:, :], c_cols), (ident[:, :], c_ident), (pos_i[:, :], positions.to_broadcast([P, SEQ]))):
                sp.dma_start(dst, src).then_inc(consts_loaded, 16)
            sp.dma_start(g_row[:, :], g_norm.to_broadcast([P, D])).then_inc(g_loaded, 16)
            for t in range(1, TOK):
                sp.dma_start(xt[:, t, :], x_v[t]).then_inc(x_loaded[t], 16)
            n0 = IDX_DIM + IDX_HEADS
            sp.dma_start(w_raw[:, 0, 0:KD * n0].rearrange("p (k n) -> p k n", k=KD),
                         w_in_v[:, :, COL_KI:COL_KI + n0]).then_inc(raw_loaded[0], 16)
            sp.dma_start(raw(1, KD), w_in_v[:, :, COL_QI:COL_QI + P]).then_inc(raw_loaded[1], 16)
            sp.wait_ge(split_done, 1)
            sp.dma_start(raw(0, KD), w_in_v[:, :, COL_QI + P:COL_QI + 2 * P]).then_inc(raw_loaded[0], 16)
            with sp.Fori(1, 4) as i:
                for half in range(2):
                    sp.wait_ge(split_done, 2 * i + half)
                    sp.dma_start(raw((1 + half) % 2, KD), w_in_v[:, :, bass.ds(2 * P * i + (COL_QI + half * P), P)]
                                 ).then_inc(raw_loaded[(1 + half) % 2], 16)
            with nc.allow_non_contiguous_dma(reason="one column per feature tile"):
                sp.dma_start(g_cols[:, 0:32], b_merge[0].rearrange("(c p) -> p c", p=P)).then_inc(ssm_loaded, 16)
                sp.dma_start(g_cols[:, 32:36], b_glu[0].rearrange("(c p) -> p c", p=P)).then_inc(ssm_loaded, 16)
                sp.dma_start(g_cols[:, 36:40], d_skip[0].rearrange("(q g) c -> (g c) q", q=QUADS)).then_inc(ssm_loaded, 16)
            sp.wait_ge(kidx_ready, 1)
            sp.dma_start(kidxT[IDX_DIM:P, :], kidxT[0:IDX_DIM, :]).then_inc(kidx_copied, 16)
            loads("k", w_in_cols(COL_K), KD)
            loads("v", w_in_cols(COL_V), KD)
            loads("u", w_in_cols(COL_U), KD)
            loads("q", w_in_cols(COL_Q), KD)
            loads("attgate", w_in_cols(COL_AG), KD)
            loads("attout", lambda i: w_att_v[:, :, bass.ds(2 * P * i, 2 * P)], 8)
            loads("merge0", w_in_cols(COL_MERGE), KD)
            loads("ssmgate", w_in_cols(COL_SG), KD)
            loads("glu", lambda i: w_glu_v, 4)
            loads("ssmout", lambda i: w_ssm_v[:, :, bass.ds(SSM_W * i, SSM_W)], 4)
            loads("merge1", w_in_cols(COL_MERGE + D), KD)
            for half in range(2):
                with sp.Fori(0, 4) as i:
                    for p in range(2):
                        slot = (UNIT0["out"] + p) % 2
                        sp.wait_ge(split_done, 2 * i + (UNIT0["out"] + 8 * half + p - 1))
                        sp.dma_start(raw(slot, 2), w_out_v[:, bass.ds(4 * i + 2 * p, 2), half * 1024:half * 1024 + 1024]
                                     ).then_inc(raw_loaded[slot], 16)
                if half == 0:
                    sp.wait_ge(gate_used, 2 * KD)
                    for t in range(TOK):
                        sp.dma_start(res[:, t, :], x_v[t]).then_inc(res_loaded, 16)
                    sp.dma_start(g_row[:, :], g_final.rearrange("(a d) -> a d", a=1).to_broadcast([P, D])
                                 ).then_inc(gf_loaded, 16)
            for t in range(TOK):
                sp.wait_ge(final_done, t + 1)
                sp.dma_start(out_v[t], res[:, t, :]).then_inc(stored, 16)
            sp.wait_ge(stored, 16 * TOK)

        @block.gpsimd
        def _(pool):
            def split(slot, u, n_el=UNIT):
                pool.tensor_scalar(w_hi[:, slot, 0:n_el], w_raw[:, slot, 0:n_el], 1.0, 1.0, ALU.mult, ALU.mult
                                   ).then_inc(high_done, 1)
                pool.wait_ge(high_done, u + 1)
                pool.tensor_tensor(w_lo[:, slot, 0:n_el], w_raw[:, slot, 0:n_el], w_hi[:, slot, 0:n_el].bitcast(F32),
                                   ALU.subtract).then_inc(split_done, 1)

            for name, n, k in SEGMENTS:
                u0 = UNIT0[name]
                for u in range(u0, u0 + min(n, 2)):
                    pool.wait_ge(raw_loaded[u % 2], 16 * (u // 2 + 1))
                    if u >= 2:
                        pool.wait_ge(tile_done, tiles_through(u - 2))
                    split(u % 2, u, KD * (IDX_DIM + IDX_HEADS) if name == "kidx" else UNIT)
                if n > 2:
                    with pool.Fori(1, n // 2) as i:
                        for half in range(2):
                            slot = (u0 + half) % 2
                            pool.wait_ge(raw_loaded[slot], 16 * i + 16 * ((u0 + half) // 2 + 1))
                            pool.wait_ge(tile_done, 2 * k * i + (TILE0[name] + (half - 1) * k))
                            pool.sem_inc(slot_claimed, 1)
                            split(slot, 2 * i + (u0 + half))

        @block.tensor
        def _(pe):
            def product(out_ap, terms, x_hi, x_lo):
                n = len(terms)
                for j, (wh, wl, k) in enumerate(terms):
                    nc.tensor.matmul(out_ap, wh, x_hi[k], start=(j == 0), stop=False)
                    nc.tensor.matmul(out_ap, wh, x_lo[k], start=False, stop=False)
                    last = nc.tensor.matmul(out_ap, wl, x_hi[k], start=False, stop=(j == n - 1))
                return last

            h_hi = [act_hi[:, k, :] for k in range(KD)]
            h_lo = [act_lo[:, k, :] for k in range(KD)]

            def project(name, x_hi, x_lo, k_n, width=P):
                per = dict((s, c) for s, _, c in SEGMENTS)[name]
                n_el = per * width

                def body(u, slot, i):
                    pe.wait_ge(split_done, u + 1)
                    for m in range(per):
                        t = (i * per) + (TILE0[name] + m)
                        parity = (TILE0[name] + (per * ((slot - UNIT0[name]) % 2)) + m) % 2
                        if not (isinstance(t, int) and t < 2):
                            pe.wait_ge(tile_free, t - 1)
                        terms = [(w_hi[:, slot, k * n_el + m * width:k * n_el + (m + 1) * width],
                                  w_lo[:, slot, k * n_el + m * width:k * n_el + (m + 1) * width], k) for k in range(k_n)]
                        out_ap = stream_bank[parity][0:width, 0:x_hi[0].shape[-1]]
                        product(out_ap, terms, x_hi, x_lo).then_inc(tile_done, 1)
                return body

            pe.wait_ge(consts_loaded, 48)
            for t in range(TOK):
                pe.wait_ge(h_ready, t + 1)
                for kq in range(4):
                    n = 4 * t + kq
                    if n >= 4:
                        pe.wait_ge(h_low, n - 3)
                    for j in range(4):
                        k = 4 * kq + j
                        last = nc.tensor.transpose(banks[4 + n % 4][:, j * P:(j + 1) * P], xt[:, t, k * P:(k + 1) * P], ident[:, :])
                    last.then_inc(h_turned, 1)
            pe.wait_ge(h_low, 16)

            project("kidx", h_hi, h_lo, KD, IDX_DIM + IDX_HEADS)(0, 0, 0)
            late_hi = [act_hi[:, k, P:SEQ] for k in range(KD)]
            late_lo = [act_lo[:, k, P:SEQ] for k in range(KD)]
            qi = project("qidx", late_hi, late_lo, KD)
            qi(1, 1, 0)
            pe.wait_ge(tile_free, 1)
            for t in range(TOK):
                last = nc.tensor.transpose(turn_bank[0][:, IDX_HEADS * t:IDX_HEADS * (t + 1)],
                                           w_idxT[IDX_DIM:IDX_DIM + IDX_HEADS, t * P:(t + 1) * P],
                                           ident[IDX_DIM:IDX_DIM + IDX_HEADS, IDX_DIM:IDX_DIM + IDX_HEADS])
            last.then_inc(wv_turned, 1)
            qi(2, 0, 1)
            with pe.Fori(1, 4) as i:
                qi(2 * i + 1, 1, 2 * i)
                qi(2 * i + 2, 0, 2 * i + 1)

            pe.wait_ge(kidx_copied, 16)
            n = 0
            for b in range(1, TOK):
                for h in range(IDX_HEADS):
                    if b == 1 and h % 2 == 0:
                        pe.wait_ge(qidx_ready, h // 2 + 1)
                    if n >= 2:
                        pe.wait_ge(relu_done, n - 1)
                    rows = slice(IDX_DIM * (h % 2), IDX_DIM * (h % 2) + IDX_DIM)
                    nc.tensor.matmul(pair_bank[n % 2][:, 0:(b + 1) * P], qidxT[rows, h // 2, (b - 1) * P:b * P],
                                     kidxT[rows, 0:(b + 1) * P], start=True, stop=True).then_inc(logit_done, 1)
                    n += 1

            unit_loop(pe, "k", project("k", h_hi, h_lo, KD))
            unit_loop(pe, "v", project("v", h_hi, h_lo, KD))
            unit_loop(pe, "u", project("u", h_hi, h_lo, KD))
            pe.wait_ge(wv_ready, 1)
            pe.wait_ge(tile_free, TILE0["v"] + KV_HEADS)
            for kv in range(KV_HEADS):
                for t in range(TOK):
                    last = nc.tensor.transpose(turn_bank[kv][:, t * P:(t + 1) * P], vT[:, kv, t * P:(t + 1) * P], ident[:, :])
            last.then_inc(wv_turned, 1)
            unit_loop(pe, "q", project("q", h_hi, h_lo, KD))
            unit_loop(pe, "attgate", project("attgate", h_hi, h_lo, KD))

            items = [(b, h) for b in range(TOK) for h in range(HEADS)]
            pe.wait_ge(qk_ready, HEADS + KV_HEADS)
            pe.wait_ge(wv_ready, 2)
            for s in range(len(items) + 3):
                if s < len(items):
                    b, h = items[s]
                    if s >= 2:
                        pe.wait_ge(masked, s - 1)
                    nc.tensor.matmul(pair_bank[s % 2][:, 0:(b + 1) * P], qT[:, h, b * P:(b + 1) * P],
                                     kT[:, h // 4, 0:(b + 1) * P], start=True, stop=True).then_inc(scores_done, 1)
                if 2 <= s < len(items) + 2:
                    i = s - 2
                    b, h = items[i]
                    pe.wait_ge(probs_ready, i + 1)
                    if i >= 2:
                        pe.wait_ge(pT_ready, i - 1)
                    for k in range(b + 1):
                        last = nc.tensor.transpose(turn_bank[i % 2][:, k * P:(k + 1) * P], probs[:, i % 3, k * P:(k + 1) * P], ident[:, :])
                    last.then_inc(p_turned, 1)
                if s >= 3:
                    i = s - 3
                    b, h = items[i]
                    pe.wait_ge(pT_ready, i + 1)
                    if i >= 2:
                        pe.wait_ge(att_ready, i - 1)
                    for k in range(b + 1):
                        last = nc.tensor.matmul(sum_bank[i % 2][:, 0:P], v_tok[:, k, (h // 4) * HD:(h // 4 + 1) * HD],
                                                pT[:, i % 2, k * P:(k + 1) * P], start=(k == 0), stop=(k == b))
                    last.then_inc(pv_done, 1)

            pe.wait_ge(a_low, HEADS)
            unit_loop(pe, "attout", project("attout", [a_hi[:, k, :] for k in range(8)], [a_lo[:, k, :] for k in range(8)], 8))

            pe.wait_ge(ssm_w_ready, 1)
            for r in range(2):
                for q in range(QUADS):
                    nc.tensor.transpose(pair_bank[r][:, q * P:(q + 1) * P],
                                        b_blk[:, r, q, :, :, :].rearrange("p a b c -> p (a b c)"), ident[:, :])
                    last = nc.tensor.transpose(turn_bank[r][:, q * P:(q + 1) * P], c_nat[:, r, q, :], ident[:, :])
            last.then_inc(ssm_w_turned, 1)
            pe.wait_ge(b_w_done, 1)
            pe.wait_ge(c_w_done, 1)

            merge0 = project("merge0", h_hi, h_lo, KD)

            def y_of(j):
                q, jj = j // 4, j % 4
                pe.wait_ge(x_ready, j + 1)
                if q >= 2 and jj == 0:
                    pe.wait_ge(y_ready, q - 1)
                out_ap = sum_bank[q % 2][32 * jj:32 * jj + 32, :]
                nc.tensor.matmul(out_ap, c_w[:, 0, q, 32 * jj:32 * jj + 32], x_ri[:, 0, :], start=True, stop=False)
                nc.tensor.matmul(out_ap, c_w[:, 1, q, 32 * jj:32 * jj + 32], x_ri[:, 1, :], start=False, stop=True
                                 ).then_inc(y_done, 1)

            for j in range(PAIRS):
                q, rows = j // 4, slice(32 * (j % 4), 32 * (j % 4) + 32)
                if j >= 1:
                    pe.wait_ge(bu_used, j)
                for r in range(2):
                    last = nc.tensor.matmul(pair_bank[r][:, :], b_w[rows, r, q, :], uT[rows, q, :], start=True, stop=True)
                last.then_inc(bu_done, 1)
                merge0(UNIT0["merge0"] + j, (UNIT0["merge0"] + j) % 2, j)
                if j >= 1:
                    y_of(j - 1)
            y_of(PAIRS - 1)

            unit_loop(pe, "ssmgate", project("ssmgate", h_hi, h_lo, KD))
            sh, sl = [s_hi[:, k, :] for k in range(4)], [s_lo[:, k, :] for k in range(4)]
            pe.wait_ge(s_ready, 4)
            unit_loop(pe, "glu", project("glu", sh, sl, 4))
            pe.wait_ge(g_ready, 4)
            unit_loop(pe, "ssmout", project("ssmout", sh, sl, 4))
            unit_loop(pe, "merge1", project("merge1", h_hi, h_lo, KD))

            for half in range(2):
                for c in range(8):
                    u = UNIT0["out"] + 8 * half + c
                    slot = u % 2
                    pe.wait_ge(split_done, u + 1)
                    if c == 0 and half == 0:
                        pe.wait_ge(tile_free, TILE0["out"])
                    if half == 0:
                        pe.wait_ge(m_low, 2 * c + 2)
                    steps = [(kt, t, n) for kt in range(2) for t in range(TOK) for n in range(2)]
                    if c == 7:
                        steps = [(kt, t, n) for t in range(TOK) for n in range(2) for kt in range(2)]
                    for kt, t, n in steps:
                        k = 2 * c + kt
                        if half == 1 and k == 0:
                            pe.wait_ge(bank_taken, 2 * t + n + 1)
                        out_ap = banks[2 * t + n][:, :]
                        mh, ml = act_hi[:, k, t * P:(t + 1) * P], act_lo[:, k, t * P:(t + 1) * P]
                        w = slice(kt * 1024 + n * 512, kt * 1024 + n * 512 + 512)
                        nc.tensor.matmul(out_ap, mh, w_hi[:, slot, w], start=(k == 0), stop=False)
                        nc.tensor.matmul(out_ap, mh, w_lo[:, slot, w], start=False, stop=False)
                        last = nc.tensor.matmul(out_ap, ml, w_hi[:, slot, w], start=False, stop=(k == KD - 1))
                        if c == 7 and kt == 1:
                            last.then_inc(bank_done, 1)
                    if c < 7:
                        last.then_inc(tile_done, 1)

        @block.scalar
        def _(act):
            count = [0]

            def link(ins):
                count[0] += 1
                ins.then_inc(a_step, 1)
                act.wait_ge(a_step, count[0])

            def copy_tile(t, dst, src, func=ACT.Copy, **kw):
                act.wait_ge(tile_done, t + 1)
                nc.scalar.activation(dst, src, func, **kw).then_inc(tile_free, 1)

            act.wait_ge(par_go, 1)
            for t in range(TOK):
                act.wait_ge(x_loaded[t], 16)
                link(nc.scalar.activation(square[:, :], xt[:, t, :], ACT.Square, accum_out=small[:, t:t + 1]))
                nc.scalar.activation(small[:, 8 + t:9 + t], small[:, t:t + 1], ACT.Sqrt, bias=small[:, 250:251], scale=1.0 / D
                                     ).then_inc(rms_done, 1)
            for t in range(TOK):
                for kq in range(4):
                    n = 4 * t + kq
                    act.wait_ge(h_turned, n + 1)
                    nc.scalar.activation(act_hi[:, 4 * kq:4 * kq + 4, t * P:(t + 1) * P],
                                         banks[4 + n % 4][:, :].rearrange("p (k n) -> p k n", k=4), ACT.Copy).then_inc(h_high, 1)
            for w in range(2):
                table = (rot_idx, rot_head)[w]
                act.wait_ge(ang_ready, w + 1)
                nc.scalar.activation(table[:, 1, :], ang[:, 0, :], ACT.Sin, scale=cols[:, 3 - 2 * w:4 - 2 * w]).then_inc(table_done, 1)
                nc.scalar.activation(table[:, 0, :], ang[:, 1, :], ACT.Sin, scale=-1.0, bias=small[:, 251:252]).then_inc(table_done, 1)

            act.wait_ge(tile_done, 1)
            nc.scalar.activation(kidxT[0:IDX_DIM, :], stream_bank[0][0:IDX_DIM, :], ACT.Copy).then_inc(kidx_raw, 1)
            nc.scalar.activation(w_idxT[IDX_DIM:IDX_DIM + IDX_HEADS, :], stream_bank[0][IDX_DIM:IDX_DIM + IDX_HEADS, :],
                                 ACT.Copy).then_inc(tile_free, 1)
            copy_tile(1, qidxT[:, 0, :], stream_bank[1][:, 0:SEQ - P])
            act.wait_ge(wv_turned, 1)
            nc.scalar.activation(w_idx[:, :, :].rearrange("p t h -> p (t h)"), turn_bank[0][:, 0:TOK * IDX_HEADS], ACT.Copy,
                                 scale=IDX_HEADS ** -0.5).then_inc(wv_ready, 1)
            for i in range(1, 8):
                copy_tile(1 + i, qidxT[:, i, :], stream_bank[(1 + i) % 2][:, 0:SEQ - P])
            n = 0
            for b in range(1, TOK):
                for h in range(IDX_HEADS):
                    act.wait_ge(logit_done, n + 1)
                    if n >= 2:
                        act.wait_ge(acc_done, n - 1)
                    nc.scalar.activation(relu[:, n % 2, 0:(b + 1) * P], pair_bank[n % 2][:, 0:(b + 1) * P], ACT.Relu,
                                         scale=IDX_DIM ** -0.5).then_inc(relu_done, 1)
                    n += 1
            for i in range(2):
                t = TILE0["k"] + i
                copy_tile(t, kT[:, i, :], stream_bank[t % 2][:, :])
            for i in range(2):
                t = TILE0["v"] + i
                copy_tile(t, vT[:, i, :], stream_bank[t % 2][:, :])
            for i in range(4):
                t = TILE0["u"] + i
                copy_tile(t, uT[:, i, :], stream_bank[t % 2][:, :])
            act.wait_ge(wv_turned, 2)
            for kv in range(KV_HEADS):
                last = nc.scalar.activation(v_tok[:, :, kv * HD:(kv + 1) * HD],
                                            turn_bank[kv][:, :].rearrange("p (t d) -> p t d", t=TOK), ACT.Copy)
            last.then_inc(wv_ready, 1)
            for i in range(HEADS):
                t = TILE0["q"] + i
                copy_tile(t, qT[:, i, :], stream_bank[t % 2][:, :])
            for i in range(HEADS):
                t = TILE0["attgate"] + i
                copy_tile(t, gate_a[:, i, :], stream_bank[t % 2][:, :], ACT.Silu)

            items = [(b, h) for b in range(TOK) for h in range(HEADS)]
            for s in range(len(items) + 2):
                if s < len(items):
                    b, h = items[s]
                    act.wait_ge(masked, s + 1)
                    act.wait_ge(nmax_ready, s + 1)
                    nc.scalar.activation(probs[:, s % 3, 0:(b + 1) * P], probs[:, s % 3, 0:(b + 1) * P], ACT.Exp,
                                         bias=small[:, 64 + s:65 + s], scale=HD ** -0.5, accum_out=small[:, 96 + s:97 + s]
                                         ).then_inc(exp_done, 1)
                if s >= 2:
                    i = s - 2
                    b, h = items[i]
                    act.wait_ge(p_turned, i + 1)
                    if i >= 2:
                        act.wait_ge(pv_done, i - 1)
                    nc.scalar.activation(pT[:, i % 2, 0:(b + 1) * P], turn_bank[i % 2][:, 0:(b + 1) * P], ACT.Copy
                                         ).then_inc(pT_ready, 1)
            for h in range(HEADS):
                act.wait_ge(att_ready, 24 + h + 1)
                nc.scalar.activation(a_hi[:, h, :], gate_a[:, h, :], ACT.Copy).then_inc(a_high, 1)
            act.wait_ge(a_low, HEADS)
            for r, src in enumerate((b_re, b_im)):
                for g in range(2):
                    act.dma_start(b_raw[STATE * g:STATE * g + STATE, r, :, :],
                                  src[0].rearrange("(j g) p c -> g p j c", g=2)[g]).then_inc(bc_loaded, 16)
            for r, src in enumerate((c_re, c_im)):
                for g in range(2):
                    act.dma_start(c_nat[:, r, :, STATE * g:STATE * g + STATE],
                                  src[0].rearrange("(q g) c p -> (g c) q p", q=QUADS)).then_inc(bc_loaded, 16)
            act.dma_start(parity[:, :], c_parity).then_inc(bc_loaded, 16)
            with nc.allow_non_contiguous_dma(reason="one column per pair of groups"):
                for g in range(2):
                    rows = slice(STATE * g, STATE * g + STATE)
                    act.dma_start(par[rows, 0, :], a_re[0].rearrange("(j g) p -> g p j", g=2)[g]).then_inc(par_loaded, 16)
                    act.dma_start(par[rows, 1, :], a_im[0].rearrange("(j g) p -> g p j", g=2)[g]).then_inc(par_loaded, 16)
                    act.dma_start(par[rows, 2, :], log_dt.rearrange("o (j g) -> g o j", g=2)[g].to_broadcast([STATE, PAIRS])
                                 ).then_inc(par_loaded, 16)
            for i in range(16):
                t = TILE0["attout"] + i
                copy_tile(t, ya[:, i, :], stream_bank[t % 2][:, :])
                if i == 1:
                    act.wait_ge(par_loaded, 6 * 16)
                    nc.scalar.activation(par[:, 3, :], par[:, 2, :], ACT.Exp).then_inc(par_done, 1)
                    act.wait_ge(par_go, 2)
                    nc.scalar.activation(par[:, 5, :], par[:, 4, :], ACT.Exp).then_inc(par_done, 1)
                    act.wait_ge(par_go, 3)
                    nc.scalar.activation(par[:, 9, :], par[:, 8, :], ACT.Sin).then_inc(par_done, 1)
                    nc.scalar.activation(par[:, 11, :], par[:, 10, :], ACT.Sin, scale=-1.0, bias=small[:, 251:252]).then_inc(par_done, 1)
            act.wait_ge(ssm_w_turned, 1)
            nc.scalar.activation(c_w[:, 0, :, :].rearrange("p q n -> p (q n)"), turn_bank[0][:, :], ACT.Copy)
            nc.scalar.activation(c_w[:, 1, :, :].rearrange("p q n -> p (q n)"), turn_bank[1][:, :], ACT.Copy, scale=-1.0
                                 ).then_inc(c_w_done, 1)

            def gelu(q):
                act.wait_ge(y_ready, q + 1)
                nc.scalar.activation(uT[:, q, :], uT[:, q, :], ACT.Gelu_apprx_tanh).then_inc(gelu_done, 1)

            for j in range(KD):
                t = TILE0["merge0"] + j
                if j >= 2:
                    act.wait_ge(gate_used, j - 1)
                if j == 0:
                    act.wait_ge(ssm_loaded, 3 * 16)
                act.wait_ge(tile_done, t + 1)
                nc.scalar.activation(gate[:, j % 2, :], stream_bank[t % 2][:, :], ACT.Sigmoid, bias=g_cols[:, j:j + 1]
                                     ).then_inc(tile_free, 1)
                if j >= 6 and (j - 6) % 4 == 0:
                    gelu((j - 6) // 4)
            gelu(3)
            act.wait_ge(y_done, PAIRS)
            for i in range(4):
                t = TILE0["ssmgate"] + i
                copy_tile(t, gate_s[:, i, :], stream_bank[t % 2][:, :], ACT.Silu)
            for i in range(4):
                t = TILE0["glu"] + i
                copy_tile(t, gate_glu[:, i, :], stream_bank[t % 2][:, :], ACT.Sigmoid, bias=g_cols[:, 32 + i:33 + i])
            for i in range(KD):
                t = TILE0["ssmout"] + i
                copy_tile(t, yb[:, i, :], stream_bank[t % 2][:, :])
            for j in range(KD):
                t = TILE0["merge1"] + j
                if KD + j >= 2:
                    act.wait_ge(gate_used, KD + j - 1)
                copy_tile(t, gate[:, j % 2, :], stream_bank[t % 2][:, :], ACT.Sigmoid, bias=g_cols[:, 16 + j:17 + j])
            act.wait_ge(tile_done, TILE0["out"])
            for j in range(KD):
                act.wait_ge(gate_used, KD + j + 1)
                nc.scalar.activation(act_hi[:, j, :], ya[:, j, :], ACT.Copy).then_inc(m_high, 1)
            n = 0
            for half in range(2):
                for t in range(TOK):
                    for c in range(2):
                        act.wait_ge(bank_taken, n + 1)
                        col = 160 + 4 * t + 2 * half + c
                        lo = half * 1024 + c * 512
                        link(nc.scalar.activation(ya[:, 0, :], res[:, t, lo:lo + 512], ACT.Square, accum_out=small[:, col:col + 1]))
                        n += 1
                    if half == 1:
                        link(nc.scalar.activation(ya[:, 1, 0:4], small[:, 160 + 4 * t:164 + 4 * t], ACT.Copy, accum_out=small[:, 180 + t:181 + t]))
                        nc.scalar.activation(small[:, 184 + t:185 + t], small[:, 180 + t:181 + t], ACT.Sqrt, bias=small[:, 250:251],
                                             scale=1.0 / D).then_inc(squares_done, 1)

        @block.vector
        def _(dve):
            v = nc.vector
            count = [0]

            def link(ins):
                count[0] += 1
                ins.then_inc(v_step, 1)
                dve.wait_ge(v_step, count[0])

            def rounded(out_ap, in_ap, factor):
                link(v.tensor_scalar(out_ap, in_ap, factor, ROUND, ALU.mult, ALU.add))
                link(v.tensor_scalar(out_ap, out_ap, ROUND, None, ALU.subtract))

            def reduce_angle(r, k):
                for turns in (4096.0, 1.0):
                    rounded(k, r, INV_2PI / turns)
                    for part in split12(2.0 * np.pi * turns):
                        link(v.scalar_tensor_tensor(r, k, -part, r, ALU.mult, ALU.add))
                link(v.tensor_scalar(r, r, PI, -PI, ALU.min, ALU.max))

            def rotate(buf, table, partner, n_rows=P, col0=0):
                n_cols = buf.shape[-1]
                t = tmp[0:n_rows, 0, 0:n_cols]
                link(v.stream_shuffle(t, buf, partner))
                link(v.tensor_tensor(t, t, table[0:n_rows, 1, col0:col0 + n_cols], ALU.mult))
                link(v.tensor_tensor(buf, buf, table[0:n_rows, 0, col0:col0 + n_cols], ALU.mult))
                return v.tensor_tensor(buf, buf, t, ALU.add)

            link(v.memset(small[:, 250:251], EPS))
            v.memset(small[:, 251:252], PI / 2).then_inc(par_go, 1)

            def low_of_h(t):
                for kq in range(4):
                    n = 4 * t + kq
                    dve.wait_ge(h_high, n + 1)
                    part = (slice(None), slice(4 * kq, 4 * kq + 4), slice(t * P, (t + 1) * P))
                    v.tensor_tensor(act_lo[part], banks[4 + n % 4][:, :].rearrange("p (k n) -> p k n", k=4),
                                    act_hi[part].bitcast(F32), ALU.subtract).then_inc(h_low, 1)

            dve.wait_ge(g_loaded, 16)
            for t in range(TOK):
                dve.wait_ge(rms_done, t + 1)
                link(v.reciprocal(small[:, 4 + t:5 + t], small[:, 8 + t:9 + t]))
                v.scalar_tensor_tensor(xt[:, t, :], xt[:, t, :], small[:, 4 + t:5 + t], g_row[:, :], ALU.mult, ALU.mult
                                       ).then_inc(h_ready, 1)
                if t >= 1:
                    low_of_h(t - 1)
            low_of_h(TOK - 1)

            dve.wait_ge(consts_loaded, 48)
            link(v.tensor_copy(pos_f[:, :], pos_i[:, :]))
            for w in range(2):
                if w == 1:
                    dve.wait_ge(table_done, 2)
                link(v.tensor_scalar(ang[:, 0, :], pos_f[:, :], cols[:, 2 - 2 * w:3 - 2 * w], None, ALU.mult))
                reduce_angle(ang[:, 0, :], tmp[:, 0, :])
                v.scalar_tensor_tensor(ang[:, 1, :], ang[:, 0, :], -1.0, ang[:, 0, :], ALU.mult, ALU.max).then_inc(ang_ready, 1)
                dve.wait_ge(ang_ready, w + 1)

            idx_partner = [q + 8 if q < 8 else q - 8 if q < 16 else q for q in range(32)]
            head_partner = [(q + 16) % 32 for q in range(32)]
            dve.wait_ge(kidx_raw, 1)
            dve.wait_ge(table_done, 2)
            rotate(kidxT[0:IDX_DIM, :], rot_idx, idx_partner, IDX_DIM).then_inc(kidx_ready, 1)
            dve.wait_ge(kidx_ready, 1)
            for i in range(8):
                dve.wait_ge(tile_free, TILE0["qidx"] + i + 1)
                rotate(qidxT[:, i, :], rot_idx, idx_partner, P, P).then_inc(qidx_ready, 1)
                dve.wait_ge(qidx_ready, i + 1)

            start = {1: 0, 2: 2 * P, 3: 5 * P}
            scores = {b: score[:, start[b]:start[b] + (b + 1) * P] for b in start}
            dve.wait_ge(wv_ready, 1)
            n = 0
            for b in range(1, TOK):
                for h in range(IDX_HEADS):
                    dve.wait_ge(relu_done, n + 1)
                    r, w = relu[:, n % 2, 0:(b + 1) * P], w_idx[:, b, h:h + 1]
                    if n:
                        dve.wait_ge(acc_done, n)
                    if h == 0:
                        ins = v.tensor_scalar(scores[b], r, w, None, ALU.mult)
                    else:
                        ins = v.scalar_tensor_tensor(scores[b], r, w, scores[b], ALU.mult, ALU.add)
                    ins.then_inc(acc_done, 1)
                    n += 1
            dve.wait_ge(acc_done, n)
            for b in range(1, TOK):
                sc = scores[b]
                link(v.memset(sc[0:CHUNK, (b + 1) * P - CHUNK:(b + 1) * P], MASKED))
                for _ in range(TOPK // 8):
                    link(v.max(small[:, 12:20], sc))
                    link(v.match_replace(sc, small[:, 12:20], sc, REPLACED))
                link(v.tensor_scalar(sc, sc, TOOK_BELOW, MASKED, ALU.is_gt, ALU.mult))
            link(v.memset(bias0[:, :], 0.0))
            link(v.memset(bias0[0:CHUNK, CHUNK:P], MASKED))
            biases = [bias0[:, :]] + [scores[b] for b in range(1, TOK)]

            for i in range(KV_HEADS):
                dve.wait_ge(tile_free, TILE0["k"] + i + 1)
                rotate(kT[:, i, :], rot_head, head_partner).then_inc(qk_ready, 1)
                dve.wait_ge(qk_ready, i + 1)
            for i in range(HEADS):
                dve.wait_ge(tile_free, TILE0["q"] + i + 1)
                rotate(qT[:, i, :], rot_head, head_partner).then_inc(qk_ready, 1)
                dve.wait_ge(qk_ready, KV_HEADS + i + 1)

            items = [(b, h) for b in range(TOK) for h in range(HEADS)]
            for s in range(len(items) + 3):
                if s < len(items):
                    b, h = items[s]
                    dve.wait_ge(scores_done, s + 1)
                    if s >= 3:
                        dve.wait_ge(p_turned, s - 2)
                    v.tensor_tensor_reduce(probs[:, s % 3, 0:(b + 1) * P], pair_bank[s % 2][:, 0:(b + 1) * P], biases[b], 1.0,
                                           REPLACED, ALU.add, ALU.max, small[:, 32 + s:33 + s]).then_inc(masked, 1)
                    dve.wait_ge(masked, s + 1)
                    v.tensor_scalar(small[:, 64 + s:65 + s], small[:, 32 + s:33 + s], -(HD ** -0.5), None, ALU.mult
                                    ).then_inc(nmax_ready, 1)
                if 1 <= s <= len(items):
                    i = s - 1
                    b, h = items[i]
                    dve.wait_ge(exp_done, i + 1)
                    link(v.reciprocal(small[:, 128 + i:129 + i], small[:, 96 + i:97 + i]))
                    pr = probs[:, i % 3, 0:(b + 1) * P]
                    v.tensor_scalar(pr, pr, small[:, 128 + i:129 + i], None, ALU.mult).then_inc(probs_ready, 1)
                if s >= 3:
                    i = s - 3
                    b, h = items[i]
                    dve.wait_ge(pv_done, i + 1)
                    if b == 0:
                        dve.wait_ge(tile_free, TILE0["attgate"] + h + 1)
                    ga = gate_a[:, h, b * P:(b + 1) * P]
                    v.tensor_tensor(ga, sum_bank[i % 2][:, 0:P], ga, ALU.mult).then_inc(att_ready, 1)
            for h in range(HEADS):
                dve.wait_ge(a_high, h + 1)
                v.tensor_tensor(a_lo[:, h, :], gate_a[:, h, :], a_hi[:, h, :].bitcast(F32), ALU.subtract).then_inc(a_low, 1)

            (AR, AI, LDT, DT, ZR, MAG, _, KT, TH, SIN, ATH, COS, LBR, LBI, DEN, RDEN, LM, T1, T2, CR, CI) = range(21)

            def p_(i):
                return par[:, i, :]

            def tt(o_, a_, b_, op):
                link(v.tensor_tensor(o_, a_, b_, op))

            dve.wait_ge(par_done, 1)
            v.tensor_tensor(p_(ZR), p_(AR), p_(DT), ALU.mult).then_inc(par_go, 1)
            tt(p_(TH), p_(AI), p_(DT), ALU.mult)
            reduce_angle(p_(TH), p_(KT))
            v.scalar_tensor_tensor(p_(ATH), p_(TH), -1.0, p_(TH), ALU.mult, ALU.max).then_inc(par_go, 1)
            dve.wait_ge(par_done, 4)
            tt(p_(LBR), p_(MAG), p_(COS), ALU.mult)
            tt(p_(LBI), p_(MAG), p_(SIN), ALU.mult)
            tt(p_(T1), p_(AR), p_(AR), ALU.mult)
            tt(p_(T2), p_(AI), p_(AI), ALU.mult)
            tt(p_(DEN), p_(T1), p_(T2), ALU.add)
            link(v.reciprocal(p_(RDEN), p_(DEN)))
            link(v.tensor_scalar(p_(LM), p_(LBR), 1.0, None, ALU.subtract))
            tt(p_(T1), p_(LM), p_(AR), ALU.mult)
            tt(p_(T2), p_(LBI), p_(AI), ALU.mult)
            tt(p_(T1), p_(T1), p_(T2), ALU.add)
            tt(p_(CR), p_(T1), p_(RDEN), ALU.mult)
            tt(p_(T1), p_(LBI), p_(AR), ALU.mult)
            tt(p_(T2), p_(LM), p_(AI), ALU.mult)
            tt(p_(T1), p_(T1), p_(T2), ALU.subtract)
            tt(p_(CI), p_(T1), p_(RDEN), ALU.mult)

            def spread(col, n_):
                return col.unsqueeze(2).to_broadcast([P, PAIRS, n_])

            dve.wait_ge(bc_loaded, 9 * 16)
            t_b = b_blk[:, 0, :, :, 0:1, :].rearrange("p q a b c -> p (q a b) c")
            for r, op in ((0, ALU.subtract), (1, ALU.add)):
                tt(b_bar[:, r, :, :], b_raw[:, r, :, :], spread(p_(CR), GCH), ALU.mult)
                tt(t_b, b_raw[:, 1 - r, :, :], spread(p_(CI), GCH), ALU.mult)
                tt(b_bar[:, r, :, :], b_bar[:, r, :, :], t_b, op)
            for r in range(2):
                for g in range(2):
                    dst = b_blk[:, r, :, :, g:g + 1, :].rearrange("p q a b c -> p (q a b) c")
                    link(v.tensor_scalar(dst, b_bar[:, r, :, :], cols[:, 4 + g:5 + g], None, ALU.mult))
            par_b = parity[:, :].unsqueeze(1).to_broadcast([P, QUADS, P])
            link(v.tensor_tensor(c_nat[:, 0, :, :], c_nat[:, 0, :, :], par_b, ALU.mult))
            v.tensor_tensor(c_nat[:, 1, :, :], c_nat[:, 1, :, :], par_b, ALU.mult).then_inc(ssm_w_ready, 1)
            dve.wait_ge(ssm_w_turned, 1)
            link(v.tensor_copy(b_w[:, 0, :, :].rearrange("p q n -> p (q n)"), pair_bank[0][:, :]))
            v.tensor_copy(b_w[:, 1, :, :].rearrange("p q n -> p (q n)"), pair_bank[1][:, :]).then_inc(b_w_done, 1)
            link(v.tensor_copy(rot[:, 0, 0, :], p_(COS)))
            link(v.tensor_copy(rot[:, 1, 0, :], p_(SIN)))
            for l in range(1, 9):
                c_, s_ = rot[:, 0, l - 1, :], rot[:, 1, l - 1, :]
                tt(p_(T1), c_, c_, ALU.mult)
                tt(p_(T2), s_, s_, ALU.mult)
                tt(rot[:, 0, l, :], p_(T1), p_(T2), ALU.subtract)
                link(v.scalar_tensor_tensor(rot[:, 1, l, :], c_, 2.0, s_, ALU.mult, ALU.mult))
            link(v.memset(e_base[:, 0, :, 0:1], 1.0))
            link(v.memset(e_base[:, 1, :, 0:1], 0.0))
            for l in range(5):
                n_ = 2 ** l
                er, ei = e_base[:, 0, :, 0:n_], e_base[:, 1, :, 0:n_]
                rr, ri = spread(rot[:, 0, l, :], n_), spread(rot[:, 1, l, :], n_)
                ta, tb = b_raw[:, 0, :, 0:n_], b_raw[:, 1, :, 0:n_]
                tt(ta, er, rr, ALU.mult)
                tt(tb, ei, ri, ALU.mult)
                tt(e_base[:, 0, :, n_:2 * n_], ta, tb, ALU.subtract)
                tt(ta, er, ri, ALU.mult)
                tt(tb, ei, rr, ALU.mult)
                tt(e_base[:, 1, :, n_:2 * n_], ta, tb, ALU.add)

            def y_of_quad(q):
                dve.wait_ge(ssm_loaded, 3 * 16)
                dve.wait_ge(y_done, 4 * q + 4)
                v.scalar_tensor_tensor(uT[:, q, :], uT[:, q, :], g_cols[:, 36 + q:37 + q], sum_bank[q % 2][:, :],
                                       ALU.mult, ALU.add).then_inc(y_ready, 1)

            for j in range(PAIRS):
                er, ei = e_tab[:, 0, :], e_tab[:, 1, :]
                link(v.tensor_copy(e_tab[:, :, 0:E_BASE], e_base[:, :, j, :]))
                for l in range(5, 9):
                    n_ = 2 ** l
                    rr, ri = rot[:, 0, l, j:j + 1], rot[:, 1, l, j:j + 1]
                    v.tensor_scalar(prod[:, 0, 0:n_], ei[:, 0:n_], ri, None, ALU.mult)
                    link(v.tensor_scalar(prod[:, 1, 0:n_], er[:, 0:n_], ri, None, ALU.mult))
                    v.scalar_tensor_tensor(er[:, n_:2 * n_], er[:, 0:n_], rr, prod[:, 0, 0:n_], ALU.mult, ALU.subtract)
                    link(v.scalar_tensor_tensor(ei[:, n_:2 * n_], ei[:, 0:n_], rr, prod[:, 1, 0:n_], ALU.mult, ALU.add))
                dve.wait_ge(bu_done, j + 1)
                br, bi = pair_bank[0][:, :], pair_bank[1][:, :]
                p0, p1, zr, zi = prod[:, 0, :], prod[:, 1, :], z_ri[:, 0, :], z_ri[:, 1, :]
                v.tensor_tensor(p0, br, er, ALU.mult)
                link(v.tensor_tensor(p1, bi, ei, ALU.mult))
                link(v.tensor_tensor(zr, p0, p1, ALU.add))
                v.tensor_tensor(p0, bi, er, ALU.mult)
                v.tensor_tensor(p1, br, ei, ALU.mult).then_inc(bu_used, 1)
                dve.wait_ge(bu_used, j + 1)
                link(v.tensor_tensor(zi, p0, p1, ALU.subtract))
                mag = p_(MAG)[:, j:j + 1].to_broadcast([P, SEQ])
                v.tensor_tensor_scan(zr, mag, zr, 0.0, ALU.mult, ALU.add)
                link(v.tensor_tensor_scan(zi, mag, zi, 0.0, ALU.mult, ALU.add))
                v.tensor_tensor(p0, zr, er, ALU.mult)
                link(v.tensor_tensor(p1, zi, ei, ALU.mult))
                if j:
                    dve.wait_ge(y_done, j)
                link(v.tensor_tensor(x_ri[:, 0, :], p0, p1, ALU.subtract))
                v.tensor_tensor(p0, zr, ei, ALU.mult)
                link(v.tensor_tensor(p1, zi, er, ALU.mult))
                v.tensor_tensor(x_ri[:, 1, :], p0, p1, ALU.add).then_inc(x_ready, 1)
                dve.wait_ge(x_ready, j + 1)
                if j >= 4 and j % 4 == 0:
                    y_of_quad(j // 4 - 1)
                dve.wait_ge(tile_free, TILE0["merge0"] + j + 1)
                v.tensor_tensor(ya[:, j, :], ya[:, j, :], gate[:, j % 2, :], ALU.mult).then_inc(gate_used, 1)
            y_of_quad(QUADS - 1)

            def split_s(k, ready):
                link(v.tensor_copy(s_hi[:, k, :], uT[:, k, :]))
                v.tensor_tensor(s_lo[:, k, :], uT[:, k, :], s_hi[:, k, :].bitcast(F32), ALU.subtract).then_inc(ready, 1)

            for k in range(QUADS):
                dve.wait_ge(gelu_done, k + 1)
                split_s(k, s_ready)
            dve.wait_ge(tile_free, TILE0["glu"] + 4)
            for k in range(QUADS):
                link(v.tensor_tensor(uT[:, k, :], uT[:, k, :], gate_glu[:, k, :], ALU.mult))
                link(v.tensor_tensor(uT[:, k, :], uT[:, k, :], gate_s[:, k, :], ALU.mult))
                split_s(k, g_ready)
            dve.wait_ge(gate_used, KD)
            for j in range(KD):
                dve.wait_ge(tile_free, TILE0["merge1"] + j + 1)
                g_ = gate[:, j % 2, :]
                link(v.tensor_tensor(g_, g_, yb[:, j, :], ALU.mult))
                v.tensor_tensor(ya[:, j, :], ya[:, j, :], g_, ALU.add).then_inc(gate_used, 1)
            for j in range(KD):
                dve.wait_ge(m_high, j + 1)
                v.tensor_tensor(act_lo[:, j, :], ya[:, j, :], act_hi[:, j, :].bitcast(F32), ALU.subtract).then_inc(m_low, 1)

            def finish(t):
                dve.wait_ge(squares_done, t + 1)
                link(v.reciprocal(small[:, 188 + t:189 + t], small[:, 184 + t:185 + t]))
                v.scalar_tensor_tensor(res[:, t, :], res[:, t, :], small[:, 188 + t:189 + t], g_row[:, :], ALU.mult, ALU.mult
                                       ).then_inc(final_done, 1)

            dve.wait_ge(res_loaded, 16 * TOK)
            dve.wait_ge(gf_loaded, 16)
            for half in range(2):
                for t in range(TOK):
                    for n in range(2):
                        dve.wait_ge(bank_done, 8 * half + 2 * t + n + 1)
                        part = res[:, t, half * 1024 + n * 512:half * 1024 + n * 512 + 512]
                        v.tensor_tensor(part, banks[2 * t + n][:, :], part, ALU.add).then_inc(bank_taken, 1)
                    if half == 1 and t >= 1:
                        finish(t - 1)
            finish(TOK - 1)


_INS = ["x", "positions", "g_norm", "w_in", "b_merge", "a_re", "a_im", "log_dt", "ssm_b_re", "ssm_b_im", "ssm_c_re",
        "ssm_c_im", "ssm_d", "w_glu", "b_glu", "w_att_out", "w_ssm_out", "w_out", "g_final"]


def kernel(**inputs):
    from concourse import bacc
    from concourse.bass_utils import run_bass_kernel_spmd

    nc = bacc.Bacc("TRN2", target_bir_lowering=False, num_devices=1)
    arrays, args = {}, []
    given = {name: np.ascontiguousarray(inputs[name]) for name in _INS} | constants()
    for name, a in given.items():
        arrays[f"in_{name}"] = a
        args.append(nc.dram_tensor(f"in_{name}", a.shape, mybir.dt.from_np(a.dtype), kind="ExternalInput").ap())
    out = nc.dram_tensor("out_dram", (1, SEQ, D), F32, kind="ExternalOutput").ap()
    hybrid_kernel(nc, *args, out)
    r = run_bass_kernel_spmd(nc, [arrays], core_ids=[0])
    return r.results[0]["out_dram"]
```

```python
from contextlib import ExitStack

import concourse.bass as bass
import numpy as np
from concourse import mybir

F32 = mybir.dt.float32
F32R = mybir.dt.float32r
I32 = mybir.dt.int32
ALU = mybir.AluOpType
ACT = mybir.ActivationFunctionType
AX_X = mybir.AxisListType.X

P = 128
SEQ = 512
D = 2048
TOK = SEQ // P
KD = D // P
EPS = 1e-6

HEADS, KV_HEADS, HD = 8, 2, 128
ATT_W, KV_W = HEADS * HD, KV_HEADS * HD
IDX_HEADS, IDX_DIM, TOPK, CHUNK = 16, 64, 128, 64
THETA = 500000.0
GROUPS, GCH, STATE = 32, 16, 64
SSM_W = GROUPS * GCH
PAIRS = GROUPS // 2
QUADS = PAIRS // 4

WIDTHS = (ATT_W, KV_W, KV_W, ATT_W, IDX_HEADS * IDX_DIM, IDX_DIM, IDX_HEADS, SSM_W, SSM_W, 2 * D)
COL_Q, COL_K, COL_V, COL_AG, COL_QI, COL_KI, COL_WI, COL_U, COL_SG, COL_MERGE = (
    int(c) for c in np.cumsum((0,) + WIDTHS[:-1]))

UNIT = 2048
REPLACED = -3.4e38
MASKED = -3.0e38
TOOK_BELOW = -3.2e38
ROUND = 1.5 * 2.0 ** 23
PI = float(np.pi)
INV_2PI = float(1.0 / (2.0 * np.pi))
E_BASE = 32

SEGMENTS = [("kidx", 1, 1), ("qidx", 8, 1), ("k", 2, 1), ("v", 2, 1), ("q", 8, 1), ("attgate", 8, 1), ("u", 4, 1),
            ("attout", 8, 2), ("merge0", 16, 1), ("ssmgate", 3, 1), ("glu", 1, 4), ("ssmgate_last", 1, 1),
            ("ssmout", 4, 4), ("merge1", 16, 1), ("out", 16, 1)]
PER_UNIT = {name: k for name, _, k in SEGMENTS}
UNIT0, TILE0 = {}, {}
_u = _t = 0
for _name, _n, _k in SEGMENTS:
    UNIT0[_name], TILE0[_name] = _u, _t
    _u, _t = _u + _n, _t + _n * _k

ITEMS_PER_UNIT = 4
ATT_STEPS = {("attgate", 6): range(0, 5), ("attgate", 7): range(5, 10),
             ("u", 0): range(10, 18), ("u", 1): range(18, 27), ("u", 2): range(27, 35)}


def split12(x):
    parts = []
    for _ in range(3):
        m, e = np.frexp(x)
        part = float(np.ldexp(np.round(m * 4096.0), e - 12))
        parts.append(part)
        x = x - part
    return parts


def constants():
    row = np.arange(P)
    freq = np.zeros((P, 6), np.float32)
    half = HD // 8
    inv = np.exp(np.float32(-np.log(THETA)) * np.arange(half, dtype=np.float32) * np.float32(2.0 / (2 * half)))
    freq[:, 0] = np.where(row < 2 * half, inv[row % half], 0)
    freq[:, 1] = np.where(row < half, -1, np.where(row < 2 * half, 1, 0))
    half = IDX_DIM // 8
    inv = np.exp(np.float32(-np.log(THETA)) * np.arange(half, dtype=np.float32) * np.float32(2.0 / (2 * half)))
    r = row % IDX_DIM
    freq[:, 2] = np.where(r < 2 * half, inv[r % half], 0)
    freq[:, 3] = np.where(r < half, -1, np.where(r < 2 * half, 1, 0))
    freq[:, 4] = row < STATE
    freq[:, 5] = row >= STATE
    parity = (row[:, None] // GCH) % 2 == (row[None, :] // STATE)
    return {"c_cols": freq, "c_ident": np.eye(P, dtype=np.float32), "c_parity": parity.astype(np.float32)}


def hybrid_kernel(nc, x, positions, g_norm, w_in, b_merge, a_re, a_im, log_dt, b_re, b_im, c_re, c_im, d_skip,
                  w_glu, b_glu, w_att_out, w_ssm_out, w_out, g_final, c_cols, c_ident, c_parity, out):
    w_in_v = w_in[0].rearrange("(k p) n -> p k n", p=P)
    w_att_v = w_att_out[0].rearrange("(k p) n -> p k n", p=P)
    w_ssm_v = w_ssm_out[0].rearrange("(k p) n -> p k n", p=P)
    w_glu_v = w_glu[0].rearrange("(k p) n -> p k n", p=P)
    w_out_v = w_out[0].rearrange("(k p) n -> p k n", p=P)
    x_v = x[0].rearrange("(t p) d -> t p d", p=P)
    out_v = out[0].rearrange("(t p) d -> t p d", p=P)

    with ExitStack() as ctx:
        base = -(-nc.sbuf_base // 32) * 32
        cursor = [base]

        def region(size):
            at = cursor[0]
            cursor[0] += size
            return at

        def at(name, offset, shape, dt=F32):
            return nc.alloc_sbuf_tensor_at(name, [P] + shape, dt, offset=offset)

        KB = 1024
        act_hi = at("act_hi", region(32 * KB), [KD, SEQ], F32R)
        act_lo = at("act_lo", region(32 * KB), [KD, SEQ], F32R)
        w_raw = at("w_raw", region(16 * KB), [2, UNIT])
        w_hi = at("w_hi", region(16 * KB), [2, UNIT], F32R)
        w_lo = at("w_lo", region(16 * KB), [2, UNIT], F32R)
        uT = at("uT", region(8 * KB), [QUADS, SEQ])
        ident = at("ident", region(KB // 2), [P])
        cols = at("cols", region(32), [6])
        g_cols = at("g_cols", region(160), [40])
        small = at("small", region(KB), [256])

        par = at("par", region(18 * 64), [18, PAIRS])
        rot = at("rot", region(KB), [2, 8, PAIRS])

        r1 = region(32 * KB)
        o = [r1]

        def take(name, shape, dt=F32):
            size = int(np.prod(shape)) * 4
            here = o[0]
            o[0] += size
            return at(name, here, shape, dt)

        rot_idx = take("rot_idx", [2, SEQ])
        rot_head = take("rot_head", [2, SEQ])
        kidxT = take("kidxT", [SEQ])
        kT = take("kT", [KV_HEADS, SEQ])
        w_idxT = at("w_idxT", o[0], [SEQ])
        v_tok = take("v_tok", [TOK, KV_W])
        tmp = take("tmp", [2, SEQ])
        w_idx = take("w_idx", [TOK, IDX_HEADS])
        relu = at("relu", o[0], [2, SEQ])
        pT = take("pT", [2, SEQ])
        vT = take("vT", [KV_HEADS, SEQ])
        pos_i = at("pos_i", o[0] - 4 * KB, [SEQ], I32)
        pos_f = at("pos_f", o[0] - 2 * KB, [SEQ])
        assert o[0] <= r1 + 32 * KB
        ya = at("ya", r1, [KD, SEQ])

        r2 = region(32 * KB)
        xt = at("xt", r2, [TOK, D])
        qidxT = at("qidxT", r2 + 16 * KB, [8, SEQ - P])
        qT = at("qT", r2, [HEADS, SEQ])
        gate_a = at("gate_a", r2 + 16 * KB, [HEADS, SEQ])
        a_hi = at("a_hi", r2, [HEADS, SEQ], F32R)
        o[0] = r2 + 16 * KB
        b_raw = take("b_raw", [2, PAIRS, GCH])
        b_bar = at("b_bar", o[0], [2, PAIRS, GCH])
        b_w = take("b_w", [2, QUADS, P])
        c_w = at("c_w", o[0], [2, QUADS, P])
        b_blk = take("b_blk", [2, QUADS, 4, 2, GCH])
        e_base = at("e_base", o[0], [2, PAIRS, E_BASE])
        c_nat = take("c_nat", [2, QUADS, P])
        parity = take("parity", [P])
        assert o[0] <= r2 + 32 * KB
        o[0] = r2
        z_ri = take("z_ri", [2, SEQ])
        prod = take("prod", [2, SEQ])
        x_ri = take("x_ri", [2, SEQ])
        assert o[0] <= r2 + 16 * KB
        gate_s = at("gate_s", r2, [QUADS, SEQ])
        gate_glu = at("gate_glu", r2 + 8 * KB, [QUADS, SEQ])
        yb = at("yb", r2, [KD, SEQ])
        res = at("res", r2, [TOK, D])

        r3 = region(16 * KB)
        g_row = at("g_row", r3, [D])
        square = at("square", r3 + 8 * KB, [D])
        o[0] = r3
        score = take("score", [P * 9])
        bias0 = take("bias0", [P])
        probs = take("probs", [3, SEQ])
        assert o[0] <= r3 + 16 * KB
        a_lo = at("a_lo", r3, [HEADS, SEQ], F32R)
        s_hi = at("s_hi", r3, [QUADS, SEQ], F32R)
        s_lo = at("s_lo", r3 + 8 * KB, [QUADS, SEQ], F32R)
        o[0] = r3
        e_tab = take("e_tab", [2, 2, SEQ])
        prod2 = take("prod2", [2, SEQ])
        e_prod = take("e_prod", [2, SEQ // 2])
        r4 = region(4 * KB)
        gate = at("gate", r4, [2, SEQ])
        ang = at("ang", r4, [2, SEQ])
        assert cursor[0] <= nc.sbuf_usable_end, cursor[0]
        nc.alloc_sbuf_tensor("arena", [P, (cursor[0] - nc.sbuf_base) // 4], F32)

        banks = [ctx.enter_context(nc.psum_tensor(f"bank{i}", [P, 512], F32)) for i in range(8)]
        stream_bank, pair_bank, turn_bank, sum_bank = banks[0:2], banks[2:4], banks[4:6], banks[6:8]

        def sem(name):
            return ctx.enter_context(nc.semaphore(name))

        raw_loaded = [sem("raw_loaded0"), sem("raw_loaded1")]
        high_done, split_done = sem("high_done"), sem("split_done")
        slot_claimed = sem("slot_claimed")
        tile_done, tile_free = sem("tile_done"), sem("tile_free")
        x_loaded = [sem(f"x_loaded{t}") for t in range(TOK)]
        consts_loaded, g_loaded, ssm_loaded = sem("consts_loaded"), sem("g_loaded"), sem("ssm_loaded")
        rms_done, h_ready, h_turned, h_high, h_low = (sem(n) for n in ("rms_done", "h_ready", "h_turned", "h_high", "h_low"))
        v_step, a_step = sem("v_step"), sem("a_step")
        ang_ready, table_done = sem("ang_ready"), sem("table_done")
        kidx_ready, kidx_copied = sem("kidx_ready"), sem("kidx_copied")
        qidx_ready, logit_done, relu_done, acc_done = (sem(n) for n in ("qidx_ready", "logit_done", "relu_done", "acc_done"))
        wv_turned, wv_ready = sem("wv_turned"), sem("wv_ready")
        qk_ready = sem("qk_ready")
        scores_done, masked, exp_done, probs_ready, p_turned, pT_ready, pv_done, att_ready = (
            sem(n) for n in ("scores_done", "masked", "exp_done", "probs_ready", "p_turned", "pT_ready", "pv_done", "att_ready"))
        a_high, a_low = sem("a_high"), sem("a_low")
        par_go, par_done = sem("par_go"), sem("par_done")
        ssm_w_ready, ssm_w_turned, c_w_done = sem("ssm_w_ready"), sem("ssm_w_turned"), sem("c_w_done")
        bu_done, bu_used, x_ready, y_done, y_ready, gelu_done = (
            sem(n) for n in ("bu_done", "bu_used", "x_ready", "y_done", "y_ready", "gelu_done"))
        gate_ready, gate_used = sem("gate_ready"), sem("gate_used")
        s_ready, g_ready, m_high, m_low = sem("s_ready"), sem("g_ready"), sem("m_high"), sem("m_low")
        bank_taken, squares_done, final_done, stored = (sem(n) for n in ("bank_taken", "squares_done", "final_done", "stored"))
        res_loaded, gf_loaded, bank_done = sem("res_loaded"), sem("gf_loaded"), sem("bank_done")
        kidx_raw, nmax_ready, bc_loaded, b_w_done, par_loaded = (
            sem(n) for n in ("kidx_raw", "nmax_ready", "bc_loaded", "b_w_done", "par_loaded"))

        block = ctx.enter_context(nc.Block())

        def tiles_through(u):
            for name, n, k in reversed(SEGMENTS):
                if u >= UNIT0[name]:
                    return TILE0[name] + (u - UNIT0[name] + 1) * k
            return 0

        def unit_loop(eng, name, body):
            n = dict((s, c) for s, c, _ in SEGMENTS)[name]
            u0 = UNIT0[name]
            if n < 4:
                for i in range(n):
                    body(u0 + i, (u0 + i) % 2, i)
                return
            with eng.Fori(0, n // 2) as i:
                for half in range(2):
                    body(u0 + half + 2 * i, (u0 + half) % 2, 2 * i + half)

        @block.sync
        def _(sp):
            def raw(slot, k):
                return w_raw[:, slot, :].rearrange("p (k n) -> p k n", k=k)

            def loads(name, source, k):
                def body(u, slot, i):
                    sp.wait_ge(split_done, u - 1)
                    sp.dma_start(raw(slot, k), source(i)).then_inc(raw_loaded[slot], 16)
                unit_loop(sp, name, body)

            def w_in_cols(col):
                return lambda i: w_in_v[:, :, bass.ds(col + P * i, P)]

            sp.dma_start(xt[:, 0, :], x_v[0]).then_inc(x_loaded[0], 16)
            for dst, src in ((cols[:, :], c_cols), (ident[:, :], c_ident), (pos_i[:, :], positions.to_broadcast([P, SEQ]))):
                sp.dma_start(dst, src).then_inc(consts_loaded, 16)
            sp.dma_start(g_row[:, :], g_norm.to_broadcast([P, D])).then_inc(g_loaded, 16)
            for t in range(1, TOK):
                sp.dma_start(xt[:, t, :], x_v[t]).then_inc(x_loaded[t], 16)
            n0 = IDX_DIM + IDX_HEADS
            sp.dma_start(w_raw[:, 0, 0:KD * n0].rearrange("p (k n) -> p k n", k=KD),
                         w_in_v[:, :, COL_KI:COL_KI + n0]).then_inc(raw_loaded[0], 16)
            sp.dma_start(raw(1, KD), w_in_v[:, :, COL_QI:COL_QI + P]).then_inc(raw_loaded[1], 16)
            sp.wait_ge(split_done, 1)
            sp.dma_start(raw(0, KD), w_in_v[:, :, COL_QI + P:COL_QI + 2 * P]).then_inc(raw_loaded[0], 16)
            with sp.Fori(1, 4) as i:
                for half in range(2):
                    sp.wait_ge(split_done, 2 * i + half)
                    sp.dma_start(raw((1 + half) % 2, KD), w_in_v[:, :, bass.ds(2 * P * i + (COL_QI + half * P), P)]
                                 ).then_inc(raw_loaded[(1 + half) % 2], 16)
            with nc.allow_non_contiguous_dma(reason="one column per feature tile"):
                sp.dma_start(g_cols[:, 0:32], b_merge[0].rearrange("(c p) -> p c", p=P)).then_inc(ssm_loaded, 16)
                sp.dma_start(g_cols[:, 32:36], b_glu[0].rearrange("(c p) -> p c", p=P)).then_inc(ssm_loaded, 16)
                sp.dma_start(g_cols[:, 36:40], d_skip[0].rearrange("(q g) c -> (g c) q", q=QUADS)).then_inc(ssm_loaded, 16)
            loads("k", w_in_cols(COL_K), KD)
            loads("v", w_in_cols(COL_V), KD)
            loads("q", w_in_cols(COL_Q), KD)
            loads("attgate", w_in_cols(COL_AG), KD)
            loads("u", w_in_cols(COL_U), KD)
            loads("attout", lambda i: w_att_v[:, :, bass.ds(2 * P * i, 2 * P)], 8)
            loads("merge0", w_in_cols(COL_MERGE), KD)
            loads("ssmgate", w_in_cols(COL_SG), KD)
            loads("glu", lambda i: w_glu_v, 4)
            loads("ssmgate_last", w_in_cols(COL_SG + 3 * P), KD)
            loads("ssmout", lambda i: w_ssm_v[:, :, bass.ds(SSM_W * i, SSM_W)], 4)
            loads("merge1", w_in_cols(COL_MERGE + D), KD)
            for half in range(2):
                with sp.Fori(0, 4) as i:
                    for p in range(2):
                        slot = (UNIT0["out"] + p) % 2
                        sp.wait_ge(split_done, 2 * i + (UNIT0["out"] + 8 * half + p - 1))
                        sp.dma_start(raw(slot, 2), w_out_v[:, bass.ds(4 * i + 2 * p, 2), half * 1024:half * 1024 + 1024]
                                     ).then_inc(raw_loaded[slot], 16)
                if half == 0:
                    sp.wait_ge(gate_used, 2 * KD)
                    for t in range(TOK):
                        sp.dma_start(res[:, t, :], x_v[t]).then_inc(res_loaded, 16)
                    sp.dma_start(g_row[:, :], g_final.rearrange("(a d) -> a d", a=1).to_broadcast([P, D])
                                 ).then_inc(gf_loaded, 16)
            for t in range(TOK):
                sp.wait_ge(final_done, t + 1)
                sp.dma_start(out_v[t], res[:, t, :]).then_inc(stored, 16)
            sp.wait_ge(stored, 16 * TOK)

        @block.gpsimd
        def _(pool):
            def split(slot, u, n_el=UNIT):
                pool.tensor_scalar(w_hi[:, slot, 0:n_el], w_raw[:, slot, 0:n_el], 1.0, 1.0, ALU.mult, ALU.mult
                                   ).then_inc(high_done, 1)
                pool.wait_ge(high_done, u + 1)
                pool.tensor_tensor(w_lo[:, slot, 0:n_el], w_raw[:, slot, 0:n_el], w_hi[:, slot, 0:n_el].bitcast(F32),
                                   ALU.subtract).then_inc(split_done, 1)

            for name, n, k in SEGMENTS:
                u0 = UNIT0[name]
                for u in range(u0, u0 + (n if n < 4 else 2)):
                    pool.wait_ge(raw_loaded[u % 2], 16 * (u // 2 + 1))
                    if u >= 2:
                        pool.wait_ge(tile_done, tiles_through(u - 2))
                    split(u % 2, u, KD * (IDX_DIM + IDX_HEADS) if name == "kidx" else UNIT)
                if n >= 4:
                    with pool.Fori(1, n // 2) as i:
                        for half in range(2):
                            slot = (u0 + half) % 2
                            pool.wait_ge(raw_loaded[slot], 16 * i + 16 * ((u0 + half) // 2 + 1))
                            pool.wait_ge(tile_done, 2 * k * i + (TILE0[name] + (half - 1) * k))
                            pool.sem_inc(slot_claimed, 1)
                            split(slot, 2 * i + (u0 + half))

        @block.tensor
        def _(pe):
            def product(out_ap, terms, x_hi, x_lo, between):
                n = len(terms)
                for j, (wh, wl, k) in enumerate(terms):
                    nc.tensor.matmul(out_ap, wh, x_hi[k], start=(j == 0), stop=False)
                    nc.tensor.matmul(out_ap, wh, x_lo[k], start=False, stop=False)
                    last = nc.tensor.matmul(out_ap, wl, x_hi[k], start=False, stop=(j == n - 1))
                    if between and j < n - 1:
                        between(j)
                return last

            h_hi = [act_hi[:, k, :] for k in range(KD)]
            h_lo = [act_lo[:, k, :] for k in range(KD)]

            def project(name, x_hi, x_lo, k_n, width=P):
                per = dict((s, c) for s, _, c in SEGMENTS)[name]
                n_el = per * width

                def body(u, slot, i, between=None):
                    pe.wait_ge(split_done, u + 1)
                    for m in range(per):
                        t = (i * per) + (TILE0[name] + m)
                        parity = (TILE0[name] + (per * ((slot - UNIT0[name]) % 2)) + m) % 2
                        if not (isinstance(t, int) and t < 2):
                            pe.wait_ge(tile_free, t - 1)
                        terms = [(w_hi[:, slot, k * n_el + m * width:k * n_el + (m + 1) * width],
                                  w_lo[:, slot, k * n_el + m * width:k * n_el + (m + 1) * width], k) for k in range(k_n)]
                        out_ap = stream_bank[parity][0:width, 0:x_hi[0].shape[-1]]
                        product(out_ap, terms, x_hi, x_lo, between).then_inc(tile_done, 1)
                return body

            pe.wait_ge(consts_loaded, 48)
            for t in range(TOK):
                pe.wait_ge(h_ready, t + 1)
                for kq in range(4):
                    n = 4 * t + kq
                    if n >= 4:
                        pe.wait_ge(h_low, n - 3)
                    for j in range(4):
                        k = 4 * kq + j
                        last = nc.tensor.transpose(banks[4 + n % 4][:, j * P:(j + 1) * P], xt[:, t, k * P:(k + 1) * P], ident[:, :])
                    last.then_inc(h_turned, 1)
            pe.wait_ge(h_low, 16)

            project("kidx", h_hi, h_lo, KD, IDX_DIM + IDX_HEADS)(0, 0, 0)
            late_hi = [act_hi[:, k, P:SEQ] for k in range(KD)]
            late_lo = [act_lo[:, k, P:SEQ] for k in range(KD)]
            qi = project("qidx", late_hi, late_lo, KD)
            qi(1, 1, 0)
            pe.wait_ge(tile_free, 1)
            for t in range(TOK):
                last = nc.tensor.transpose(turn_bank[0][:, IDX_HEADS * t:IDX_HEADS * (t + 1)],
                                           w_idxT[IDX_DIM:IDX_DIM + IDX_HEADS, t * P:(t + 1) * P],
                                           ident[IDX_DIM:IDX_DIM + IDX_HEADS, IDX_DIM:IDX_DIM + IDX_HEADS])
            last.then_inc(wv_turned, 1)
            qi(2, 0, 1)
            with pe.Fori(1, 4) as i:
                qi(2 * i + 1, 1, 2 * i)
                qi(2 * i + 2, 0, 2 * i + 1)

            idx_items = [(b, h) for b in range(1, TOK) for h in range(IDX_HEADS)]

            def indexer_item(n):
                b, h = idx_items[n]
                if n == 0:
                    pe.wait_ge(kidx_copied, 16)
                if b == 1 and h % 2 == 0:
                    pe.wait_ge(qidx_ready, h // 2 + 1)
                if n >= 2:
                    pe.wait_ge(relu_done, n - 1)
                rows = slice(IDX_DIM * (h % 2), IDX_DIM * (h % 2) + IDX_DIM)
                nc.tensor.matmul(pair_bank[n % 2][:, 0:(b + 1) * P], qidxT[rows, h // 2, (b - 1) * P:b * P],
                                 kidxT[rows, 0:(b + 1) * P], start=True, stop=True).then_inc(logit_done, 1)

            done = 0
            for name, count in (("k", 2), ("v", 2), ("q", 8)):
                unit = project(name, h_hi, h_lo, KD)
                for i in range(count):
                    first = ITEMS_PER_UNIT * done
                    unit(UNIT0[name] + i, (UNIT0[name] + i) % 2, i,
                         lambda k: indexer_item(first + k // 4) if k % 4 == 2 else None)
                    done += 1
                    if (name, i) == ("q", 0):
                        pe.wait_ge(wv_ready, 1)
                        pe.wait_ge(tile_free, TILE0["v"] + KV_HEADS)
                        for kv in range(KV_HEADS):
                            for t in range(TOK):
                                last = nc.tensor.transpose(turn_bank[kv][:, t * P:(t + 1) * P], vT[:, kv, t * P:(t + 1) * P],
                                                           ident[:, :])
                        last.then_inc(wv_turned, 1)

            items = [(b, h) for b in range(TOK) for h in range(HEADS)]

            def attention_step(s):
                if s == 0:
                    pe.wait_ge(qk_ready, HEADS + KV_HEADS)
                    pe.wait_ge(wv_ready, 2)
                if s < len(items):
                    b, h = items[s]
                    if s >= 2:
                        pe.wait_ge(masked, s - 1)
                    nc.tensor.matmul(pair_bank[s % 2][:, 0:(b + 1) * P], qT[:, h, b * P:(b + 1) * P],
                                     kT[:, h // 4, 0:(b + 1) * P], start=True, stop=True).then_inc(scores_done, 1)
                if 2 <= s < len(items) + 2:
                    i = s - 2
                    b, h = items[i]
                    pe.wait_ge(probs_ready, i + 1)
                    if i >= 2:
                        pe.wait_ge(pT_ready, i - 1)
                    for k in range(b + 1):
                        last = nc.tensor.transpose(turn_bank[i % 2][:, k * P:(k + 1) * P], probs[:, i % 3, k * P:(k + 1) * P],
                                                   ident[:, :])
                    last.then_inc(p_turned, 1)
                if s >= 3:
                    i = s - 3
                    b, h = items[i]
                    pe.wait_ge(pT_ready, i + 1)
                    if i >= 2:
                        pe.wait_ge(att_ready, i - 1)
                    for k in range(b + 1):
                        last = nc.tensor.matmul(sum_bank[i % 2][:, 0:P], v_tok[:, k, (h // 4) * HD:(h // 4 + 1) * HD],
                                                pT[:, i % 2, k * P:(k + 1) * P], start=(k == 0), stop=(k == b))
                    last.then_inc(pv_done, 1)

            attgate = project("attgate", h_hi, h_lo, KD)
            with pe.Fori(0, 3) as i:
                for half in range(2):
                    attgate(2 * i + (UNIT0["attgate"] + half), (UNIT0["attgate"] + half) % 2, 2 * i + half)
            for name, i in (("attgate", 6), ("attgate", 7), ("u", 0), ("u", 1), ("u", 2), ("u", 3)):
                steps = ATT_STEPS.get((name, i), range(0))
                behind = {(KD - 1) * (n + 1) // len(steps) - 1: s for n, s in enumerate(steps)}
                project(name, h_hi, h_lo, KD)(UNIT0[name] + i, (UNIT0[name] + i) % 2, i,
                                              lambda k: attention_step(behind[k]) if k in behind else None)

            pe.wait_ge(a_low, HEADS)
            attout = project("attout", [a_hi[:, k, :] for k in range(8)], [a_lo[:, k, :] for k in range(8)], 8)
            u0 = UNIT0["attout"]
            with pe.Fori(0, 3) as i:
                for half in range(2):
                    attout(2 * i + (u0 + half), (u0 + half) % 2, 2 * i + half)

            pe.wait_ge(ssm_w_ready, 1)
            for r in range(2):
                for q in range(QUADS):
                    nc.tensor.transpose(pair_bank[r][:, q * P:(q + 1) * P],
                                        b_blk[:, r, q, :, :, :].rearrange("p a b c -> p (a b c)"), ident[:, :])
                    last = nc.tensor.transpose(turn_bank[r][:, q * P:(q + 1) * P], c_nat[:, r, q, :], ident[:, :])
            last.then_inc(ssm_w_turned, 1)
            for i in (6, 7):
                attout(u0 + i, (u0 + i) % 2, i)
            pe.wait_ge(b_w_done, 1)
            pe.wait_ge(c_w_done, 1)

            merge0 = project("merge0", h_hi, h_lo, KD)

            def y_of(j):
                q, jj = j // 4, j % 4
                pe.wait_ge(x_ready, j + 1)
                if q >= 2 and jj == 0:
                    pe.wait_ge(y_ready, q - 1)
                out_ap = sum_bank[q % 2][32 * jj:32 * jj + 32, :]
                nc.tensor.matmul(out_ap, c_w[:, 0, q, 32 * jj:32 * jj + 32], x_ri[:, 0, :], start=True, stop=False)
                nc.tensor.matmul(out_ap, c_w[:, 1, q, 32 * jj:32 * jj + 32], x_ri[:, 1, :], start=False, stop=True
                                 ).then_inc(y_done, 1)

            for j in range(PAIRS):
                q, rows = j // 4, slice(32 * (j % 4), 32 * (j % 4) + 32)
                if j >= 1:
                    pe.wait_ge(bu_used, j)
                for r in range(2):
                    last = nc.tensor.matmul(pair_bank[r][:, :], b_w[rows, r, q, :], uT[rows, q, :], start=True, stop=True)
                last.then_inc(bu_done, 1)
                merge0(UNIT0["merge0"] + j, (UNIT0["merge0"] + j) % 2, j)
                if j >= 1:
                    y_of(j - 1)
            ssmgate = project("ssmgate", h_hi, h_lo, KD)
            for i in range(3):
                if i == 2:
                    y_of(PAIRS - 1)
                ssmgate(UNIT0["ssmgate"] + i, (UNIT0["ssmgate"] + i) % 2, i)
            sh, sl = [s_hi[:, k, :] for k in range(4)], [s_lo[:, k, :] for k in range(4)]
            pe.wait_ge(s_ready, 4)
            unit_loop(pe, "glu", project("glu", sh, sl, 4))
            unit_loop(pe, "ssmgate_last", project("ssmgate_last", h_hi, h_lo, KD))
            pe.wait_ge(g_ready, 4)
            unit_loop(pe, "ssmout", project("ssmout", sh, sl, 4))
            unit_loop(pe, "merge1", project("merge1", h_hi, h_lo, KD))

            for half in range(2):
                for c in range(8):
                    u = UNIT0["out"] + 8 * half + c
                    slot = u % 2
                    pe.wait_ge(split_done, u + 1)
                    if c == 0 and half == 0:
                        pe.wait_ge(tile_free, TILE0["out"])
                    if half == 0:
                        pe.wait_ge(m_low, 2 * c + 2)
                    steps = [(kt, t, n) for kt in range(2) for t in range(TOK) for n in range(2)]
                    if c == 7:
                        steps = [(kt, t, n) for t in range(TOK) for n in range(2) for kt in range(2)]
                    for kt, t, n in steps:
                        k = 2 * c + kt
                        if half == 1 and k == 0:
                            pe.wait_ge(bank_taken, 2 * t + n + 1)
                        out_ap = banks[2 * t + n][:, :]
                        mh, ml = act_hi[:, k, t * P:(t + 1) * P], act_lo[:, k, t * P:(t + 1) * P]
                        w = slice(kt * 1024 + n * 512, kt * 1024 + n * 512 + 512)
                        nc.tensor.matmul(out_ap, mh, w_hi[:, slot, w], start=(k == 0), stop=False)
                        nc.tensor.matmul(out_ap, mh, w_lo[:, slot, w], start=False, stop=False)
                        last = nc.tensor.matmul(out_ap, ml, w_hi[:, slot, w], start=False, stop=(k == KD - 1))
                        if c == 7 and kt == 1 and (t, n) != (TOK - 1, 1):
                            last.then_inc(bank_done, 1)
                    last.then_inc(tile_done, 1)

        @block.scalar
        def _(act):
            count = [0]

            def link(ins):
                count[0] += 1
                ins.then_inc(a_step, 1)
                act.wait_ge(a_step, count[0])

            def copy_tile(t, dst, src, func=ACT.Copy, **kw):
                act.wait_ge(tile_done, t + 1)
                nc.scalar.activation(dst, src, func, **kw).then_inc(tile_free, 1)

            act.wait_ge(par_go, 1)
            for t in range(TOK):
                act.wait_ge(x_loaded[t], 16)
                link(nc.scalar.activation(square[:, :], xt[:, t, :], ACT.Square, accum_out=small[:, t:t + 1]))
                nc.scalar.activation(small[:, 8 + t:9 + t], small[:, t:t + 1], ACT.Sqrt, bias=small[:, 250:251], scale=1.0 / D
                                     ).then_inc(rms_done, 1)
            for t in range(TOK):
                for kq in range(4):
                    n = 4 * t + kq
                    act.wait_ge(h_turned, n + 1)
                    nc.scalar.activation(act_hi[:, 4 * kq:4 * kq + 4, t * P:(t + 1) * P],
                                         banks[4 + n % 4][:, :].rearrange("p (k n) -> p k n", k=4), ACT.Copy).then_inc(h_high, 1)
            for w in range(2):
                table = (rot_idx, rot_head)[w]
                act.wait_ge(ang_ready, w + 1)
                nc.scalar.activation(table[:, 1, :], ang[:, 0, :], ACT.Sin, scale=cols[:, 3 - 2 * w:4 - 2 * w]).then_inc(table_done, 1)
                nc.scalar.activation(table[:, 0, :], ang[:, 1, :], ACT.Sin, scale=-1.0, bias=small[:, 251:252]).then_inc(table_done, 1)

            act.wait_ge(tile_done, 1)
            nc.scalar.activation(kidxT[0:IDX_DIM, :], stream_bank[0][0:IDX_DIM, :], ACT.Copy).then_inc(kidx_raw, 1)
            nc.scalar.activation(w_idxT[IDX_DIM:IDX_DIM + IDX_HEADS, :], stream_bank[0][IDX_DIM:IDX_DIM + IDX_HEADS, :],
                                 ACT.Copy).then_inc(tile_free, 1)
            copy_tile(1, qidxT[:, 0, :], stream_bank[1][:, 0:SEQ - P])
            act.wait_ge(wv_turned, 1)
            nc.scalar.activation(w_idx[:, :, :].rearrange("p t h -> p (t h)"), turn_bank[0][:, 0:TOK * IDX_HEADS], ACT.Copy,
                                 scale=IDX_HEADS ** -0.5).then_inc(wv_ready, 1)
            for i in range(1, 8):
                copy_tile(1 + i, qidxT[:, i, :], stream_bank[(1 + i) % 2][:, 0:SEQ - P])
                if i == 1:
                    act.wait_ge(kidx_ready, 1)
                    act.dma_start(kidxT[IDX_DIM:P, :], kidxT[0:IDX_DIM, :]).then_inc(kidx_copied, 16)
            with nc.allow_non_contiguous_dma(reason="one column per pair of groups"):
                for g in range(2):
                    rows = slice(STATE * g, STATE * g + STATE)
                    act.dma_start(par[rows, 0, :], a_re[0].rearrange("(j g) p -> g p j", g=2)[g]).then_inc(par_loaded, 16)
                    act.dma_start(par[rows, 1, :], a_im[0].rearrange("(j g) p -> g p j", g=2)[g]).then_inc(par_loaded, 16)
                    act.dma_start(par[rows, 2, :], log_dt.rearrange("o (j g) -> g o j", g=2)[g].to_broadcast([STATE, PAIRS])
                                  ).then_inc(par_loaded, 16)
            n = 0
            for dst in [kT[:, i, :] for i in range(2)] + [vT[:, i, :] for i in range(2)] + [qT[:, i, :] for i in range(8)]:
                for _ in range(ITEMS_PER_UNIT):
                    b = 1 + n // IDX_HEADS
                    act.wait_ge(logit_done, n + 1)
                    if n >= 2:
                        act.wait_ge(acc_done, n - 1)
                    nc.scalar.activation(relu[:, n % 2, 0:(b + 1) * P], pair_bank[n % 2][:, 0:(b + 1) * P], ACT.Relu,
                                         scale=IDX_DIM ** -0.5).then_inc(relu_done, 1)
                    n += 1
                t = TILE0["k"] + n // ITEMS_PER_UNIT - 1
                copy_tile(t, dst, stream_bank[t % 2][:, :])
                if t == TILE0["q"]:
                    act.wait_ge(wv_turned, 2)
                    for kv in range(KV_HEADS):
                        last = nc.scalar.activation(v_tok[:, :, kv * HD:(kv + 1) * HD],
                                                    turn_bank[kv][:, :].rearrange("p (t d) -> p t d", t=TOK), ACT.Copy)
                    last.then_inc(wv_ready, 1)

            items = [(b, h) for b in range(TOK) for h in range(HEADS)]

            def attention_step(s):
                if s < len(items):
                    b, h = items[s]
                    act.wait_ge(masked, s + 1)
                    act.wait_ge(nmax_ready, s + 1)
                    nc.scalar.activation(probs[:, s % 3, 0:(b + 1) * P], probs[:, s % 3, 0:(b + 1) * P], ACT.Exp,
                                         bias=small[:, 64 + s:65 + s], scale=HD ** -0.5, accum_out=small[:, 96 + s:97 + s]
                                         ).then_inc(exp_done, 1)
                if 2 <= s < len(items) + 2:
                    i = s - 2
                    b, h = items[i]
                    act.wait_ge(p_turned, i + 1)
                    if i >= 2:
                        act.wait_ge(pv_done, i - 1)
                    nc.scalar.activation(pT[:, i % 2, 0:(b + 1) * P], turn_bank[i % 2][:, 0:(b + 1) * P], ACT.Copy
                                         ).then_inc(pT_ready, 1)

            for i in range(HEADS):
                for s in ATT_STEPS.get(("attgate", i), ()):
                    attention_step(s)
                t = TILE0["attgate"] + i
                copy_tile(t, gate_a[:, i, :], stream_bank[t % 2][:, :], ACT.Silu)
                if i == 4:
                    act.wait_ge(par_loaded, 6 * 16)
                    nc.scalar.activation(par[:, 3, :], par[:, 2, :], ACT.Exp).then_inc(par_done, 1)
                    act.wait_ge(par_go, 2)
                    nc.scalar.activation(par[:, 5, :], par[:, 4, :], ACT.Exp).then_inc(par_done, 1)
                    act.wait_ge(par_go, 3)
                    nc.scalar.activation(par[:, 9, :], par[:, 8, :], ACT.Sin).then_inc(par_done, 1)
                    nc.scalar.activation(par[:, 11, :], par[:, 10, :], ACT.Sin, scale=-1.0, bias=small[:, 251:252]
                                         ).then_inc(par_done, 1)
            for i in range(QUADS):
                for s in ATT_STEPS.get(("u", i), ()):
                    attention_step(s)
                if i == QUADS - 1:
                    for h in range(HEADS):
                        act.wait_ge(att_ready, 24 + h + 1)
                        nc.scalar.activation(a_hi[:, h, :], gate_a[:, h, :], ACT.Copy).then_inc(a_high, 1)
                t = TILE0["u"] + i
                copy_tile(t, uT[:, i, :], stream_bank[t % 2][:, :])
            act.wait_ge(a_low, HEADS)
            for r, src in enumerate((b_re, b_im)):
                for g in range(2):
                    act.dma_start(b_raw[STATE * g:STATE * g + STATE, r, :, :],
                                  src[0].rearrange("(j g) p c -> g p j c", g=2)[g]).then_inc(bc_loaded, 16)
            for r, src in enumerate((c_re, c_im)):
                for g in range(2):
                    act.dma_start(c_nat[:, r, :, STATE * g:STATE * g + STATE],
                                  src[0].rearrange("(q g) c p -> (g c) q p", q=QUADS)).then_inc(bc_loaded, 16)
            act.dma_start(parity[:, :], c_parity).then_inc(bc_loaded, 16)
            for i in range(16):
                t = TILE0["attout"] + i
                copy_tile(t, ya[:, i, :], stream_bank[t % 2][:, :])
                if i == 11:
                    act.wait_ge(ssm_w_turned, 1)
                    nc.scalar.activation(c_w[:, 0, :, :].rearrange("p q n -> p (q n)"), turn_bank[0][:, :], ACT.Copy)
                    nc.scalar.activation(c_w[:, 1, :, :].rearrange("p q n -> p (q n)"), turn_bank[1][:, :], ACT.Copy, scale=-1.0
                                         ).then_inc(c_w_done, 1)

            def gelu(q):
                act.wait_ge(y_ready, q + 1)
                nc.scalar.activation(uT[:, q, :], uT[:, q, :], ACT.Gelu_apprx_tanh).then_inc(gelu_done, 1)

            for j in range(KD):
                t = TILE0["merge0"] + j
                if j >= 2:
                    act.wait_ge(gate_used, j - 1)
                if j == 0:
                    act.wait_ge(ssm_loaded, 3 * 16)
                act.wait_ge(tile_done, t + 1)
                nc.scalar.activation(gate[:, j % 2, :], stream_bank[t % 2][:, :], ACT.Sigmoid, bias=g_cols[:, j:j + 1]
                                     ).then_inc(tile_free, 1)
                if j >= 6 and (j - 6) % 4 == 0:
                    gelu((j - 6) // 4)
            act.wait_ge(x_ready, PAIRS)
            for i in range(3):
                if i == 2:
                    gelu(3)
                t = TILE0["ssmgate"] + i
                copy_tile(t, gate_s[:, i, :], stream_bank[t % 2][:, :], ACT.Silu)
            for i in range(4):
                t = TILE0["glu"] + i
                copy_tile(t, gate_glu[:, i, :], stream_bank[t % 2][:, :], ACT.Sigmoid, bias=g_cols[:, 32 + i:33 + i])
            t = TILE0["ssmgate_last"]
            copy_tile(t, gate_s[:, 3, :], stream_bank[t % 2][:, :], ACT.Silu)
            for i in range(KD):
                t = TILE0["ssmout"] + i
                copy_tile(t, yb[:, i, :], stream_bank[t % 2][:, :])
            for j in range(KD):
                t = TILE0["merge1"] + j
                if KD + j >= 2:
                    act.wait_ge(gate_used, KD + j - 1)
                copy_tile(t, gate[:, j % 2, :], stream_bank[t % 2][:, :], ACT.Sigmoid, bias=g_cols[:, 16 + j:17 + j])
            act.wait_ge(tile_done, TILE0["out"])
            for j in range(KD):
                act.wait_ge(gate_used, KD + j + 1)
                nc.scalar.activation(act_hi[:, j, :], ya[:, j, :], ACT.Copy).then_inc(m_high, 1)
            n = 0
            for half in range(2):
                for t in range(TOK):
                    for c in range(2):
                        act.wait_ge(bank_taken, n + 1)
                        col = 160 + 4 * t + 2 * half + c
                        lo = half * 1024 + c * 512
                        link(nc.scalar.activation(ya[:, 0, :], res[:, t, lo:lo + 512], ACT.Square, accum_out=small[:, col:col + 1]))
                        n += 1
                    if half == 1:
                        link(nc.scalar.activation(ya[:, 1, 0:4], small[:, 160 + 4 * t:164 + 4 * t], ACT.Copy, accum_out=small[:, 180 + t:181 + t]))
                        nc.scalar.activation(small[:, 184 + t:185 + t], small[:, 180 + t:181 + t], ACT.Sqrt, bias=small[:, 250:251],
                                             scale=1.0 / D).then_inc(squares_done, 1)

        @block.vector
        def _(dve):
            v = nc.vector
            count = [0]

            def link(ins):
                count[0] += 1
                ins.then_inc(v_step, 1)
                dve.wait_ge(v_step, count[0])

            def rounded(out_ap, in_ap, factor):
                link(v.tensor_scalar(out_ap, in_ap, factor, ROUND, ALU.mult, ALU.add))
                link(v.tensor_scalar(out_ap, out_ap, ROUND, None, ALU.subtract))

            def reduce_angle(r, k):
                for turns in (4096.0, 1.0):
                    rounded(k, r, INV_2PI / turns)
                    for part in split12(2.0 * np.pi * turns):
                        link(v.scalar_tensor_tensor(r, k, -part, r, ALU.mult, ALU.add))
                link(v.tensor_scalar(r, r, PI, -PI, ALU.min, ALU.max))

            def rotate(buf, table, partner, n_rows=P, col0=0):
                n_cols = buf.shape[-1]
                t = tmp[0:n_rows, 0, 0:n_cols]
                link(v.stream_shuffle(t, buf, partner))
                link(v.tensor_tensor(t, t, table[0:n_rows, 1, col0:col0 + n_cols], ALU.mult))
                link(v.tensor_tensor(buf, buf, table[0:n_rows, 0, col0:col0 + n_cols], ALU.mult))
                return v.tensor_tensor(buf, buf, t, ALU.add)

            link(v.memset(small[:, 250:251], EPS))
            v.memset(small[:, 251:252], PI / 2).then_inc(par_go, 1)

            def low_of_h(t):
                for kq in range(4):
                    n = 4 * t + kq
                    dve.wait_ge(h_high, n + 1)
                    part = (slice(None), slice(4 * kq, 4 * kq + 4), slice(t * P, (t + 1) * P))
                    v.tensor_tensor(act_lo[part], banks[4 + n % 4][:, :].rearrange("p (k n) -> p k n", k=4),
                                    act_hi[part].bitcast(F32), ALU.subtract).then_inc(h_low, 1)

            dve.wait_ge(g_loaded, 16)
            for t in range(TOK):
                dve.wait_ge(rms_done, t + 1)
                link(v.reciprocal(small[:, 4 + t:5 + t], small[:, 8 + t:9 + t]))
                v.scalar_tensor_tensor(xt[:, t, :], xt[:, t, :], small[:, 4 + t:5 + t], g_row[:, :], ALU.mult, ALU.mult
                                       ).then_inc(h_ready, 1)
                if t >= 1:
                    low_of_h(t - 1)
            low_of_h(TOK - 1)

            dve.wait_ge(consts_loaded, 48)
            link(v.tensor_copy(pos_f[:, :], pos_i[:, :]))
            for w in range(2):
                if w == 1:
                    dve.wait_ge(table_done, 2)
                link(v.tensor_scalar(ang[:, 0, :], pos_f[:, :], cols[:, 2 - 2 * w:3 - 2 * w], None, ALU.mult))
                reduce_angle(ang[:, 0, :], tmp[:, 0, :])
                v.scalar_tensor_tensor(ang[:, 1, :], ang[:, 0, :], -1.0, ang[:, 0, :], ALU.mult, ALU.max).then_inc(ang_ready, 1)
                dve.wait_ge(ang_ready, w + 1)

            idx_partner = [q + 8 if q < 8 else q - 8 if q < 16 else q for q in range(32)]
            head_partner = [(q + 16) % 32 for q in range(32)]
            dve.wait_ge(kidx_raw, 1)
            dve.wait_ge(table_done, 2)
            rotate(kidxT[0:IDX_DIM, :], rot_idx, idx_partner, IDX_DIM).then_inc(kidx_ready, 1)
            dve.wait_ge(kidx_ready, 1)
            for i in range(8):
                dve.wait_ge(tile_free, TILE0["qidx"] + i + 1)
                rotate(qidxT[:, i, :], rot_idx, idx_partner, P, P).then_inc(qidx_ready, 1)
                dve.wait_ge(qidx_ready, i + 1)

            start = {1: 0, 2: 2 * P, 3: 5 * P}
            scores = {b: score[:, start[b]:start[b] + (b + 1) * P] for b in start}
            dve.wait_ge(wv_ready, 1)

            def add_item(n):
                b, h = 1 + n // IDX_HEADS, n % IDX_HEADS
                dve.wait_ge(relu_done, n + 1)
                r, w = relu[:, n % 2, 0:(b + 1) * P], w_idx[:, b, h:h + 1]
                if h == 0:
                    ins = v.tensor_scalar(scores[b], r, w, None, ALU.mult)
                else:
                    ins = v.scalar_tensor_tensor(scores[b], r, w, scores[b], ALU.mult, ALU.add)
                ins.then_inc(acc_done, 1)
                dve.wait_ge(acc_done, n + 1)

            def open_topk(b):
                link(v.memset(scores[b][0:CHUNK, (b + 1) * P - CHUNK:(b + 1) * P], MASKED))

            def topk_round(b):
                link(v.max(small[:, 12:20], scores[b]))
                link(v.match_replace(scores[b], small[:, 12:20], scores[b], REPLACED))

            def close_topk(b):
                link(v.tensor_scalar(scores[b], scores[b], TOOK_BELOW, MASKED, ALU.is_gt, ALU.mult))

            n = 0
            for b in range(1, TOK):
                for h in range(IDX_HEADS):
                    add_item(n)
                    if b > 1:
                        topk_round(b - 1)
                    n += 1
                    if n % ITEMS_PER_UNIT == 0:
                        unit = n // ITEMS_PER_UNIT - 1
                        t = TILE0["k"] + unit
                        if unit < 2 or unit >= 4:
                            dve.wait_ge(tile_free, t + 1)
                            buf = kT[:, unit, :] if unit < 2 else qT[:, unit - 4, :]
                            rotate(buf, rot_head, head_partner).then_inc(qk_ready, 1)
                            dve.wait_ge(qk_ready, unit + 1 if unit < 2 else unit - 1)
                if b > 1:
                    close_topk(b - 1)
                open_topk(b)
            for _ in range(TOPK // 8):
                topk_round(TOK - 1)
            close_topk(TOK - 1)
            link(v.memset(bias0[:, :], 0.0))
            link(v.memset(bias0[0:CHUNK, CHUNK:P], MASKED))
            biases = [bias0[:, :]] + [scores[b] for b in range(1, TOK)]

            (AR, AI, LDT, DT, ZR, MAG, KT, LBR, TH, SIN, ATH, COS, LBI, DEN, T1, T2, CR, CI) = range(18)
            RDEN, LM = LDT, DT

            def p_(i):
                return par[:, i, :]

            def tt(o_, a_, b_, op):
                link(v.tensor_tensor(o_, a_, b_, op))

            dve.wait_ge(par_done, 1)
            v.tensor_tensor(p_(ZR), p_(AR), p_(DT), ALU.mult).then_inc(par_go, 1)
            tt(p_(TH), p_(AI), p_(DT), ALU.mult)
            reduce_angle(p_(TH), p_(KT))
            v.scalar_tensor_tensor(p_(ATH), p_(TH), -1.0, p_(TH), ALU.mult, ALU.max).then_inc(par_go, 1)
            dve.wait_ge(par_done, 4)
            tt(p_(LBR), p_(MAG), p_(COS), ALU.mult)
            tt(p_(LBI), p_(MAG), p_(SIN), ALU.mult)
            tt(p_(T1), p_(AR), p_(AR), ALU.mult)
            tt(p_(T2), p_(AI), p_(AI), ALU.mult)
            tt(p_(DEN), p_(T1), p_(T2), ALU.add)
            link(v.reciprocal(p_(RDEN), p_(DEN)))
            link(v.tensor_scalar(p_(LM), p_(LBR), 1.0, None, ALU.subtract))
            tt(p_(T1), p_(LM), p_(AR), ALU.mult)
            tt(p_(T2), p_(LBI), p_(AI), ALU.mult)
            tt(p_(T1), p_(T1), p_(T2), ALU.add)
            tt(p_(CR), p_(T1), p_(RDEN), ALU.mult)
            tt(p_(T1), p_(LBI), p_(AR), ALU.mult)
            tt(p_(T2), p_(LM), p_(AI), ALU.mult)
            tt(p_(T1), p_(T1), p_(T2), ALU.subtract)
            tt(p_(CI), p_(T1), p_(RDEN), ALU.mult)

            rotors = [(p_(COS), p_(SIN))] + [(rot[:, 0, l, :], rot[:, 1, l, :]) for l in range(8)]
            for (c_, s_), (c2, s2) in zip(rotors, rotors[1:]):
                tt(p_(T1), c_, c_, ALU.mult)
                tt(p_(T2), s_, s_, ALU.mult)
                tt(c2, p_(T1), p_(T2), ALU.subtract)
                link(v.scalar_tensor_tensor(s2, c_, 2.0, s_, ALU.mult, ALU.mult))

            items = [(b, h) for b in range(TOK) for h in range(HEADS)]
            for s in range(len(items) + 3):
                if s < len(items):
                    b, h = items[s]
                    dve.wait_ge(scores_done, s + 1)
                    if s >= 3:
                        dve.wait_ge(p_turned, s - 2)
                    v.tensor_tensor_reduce(probs[:, s % 3, 0:(b + 1) * P], pair_bank[s % 2][:, 0:(b + 1) * P], biases[b], 1.0,
                                           REPLACED, ALU.add, ALU.max, small[:, 32 + s:33 + s]).then_inc(masked, 1)
                    dve.wait_ge(masked, s + 1)
                    v.tensor_scalar(small[:, 64 + s:65 + s], small[:, 32 + s:33 + s], -(HD ** -0.5), None, ALU.mult
                                    ).then_inc(nmax_ready, 1)
                if 1 <= s <= len(items):
                    i = s - 1
                    b, h = items[i]
                    dve.wait_ge(exp_done, i + 1)
                    link(v.reciprocal(small[:, 128 + i:129 + i], small[:, 96 + i:97 + i]))
                    pr = probs[:, i % 3, 0:(b + 1) * P]
                    v.tensor_scalar(pr, pr, small[:, 128 + i:129 + i], None, ALU.mult).then_inc(probs_ready, 1)
                if s >= 3:
                    i = s - 3
                    b, h = items[i]
                    dve.wait_ge(pv_done, i + 1)
                    if b == 0:
                        dve.wait_ge(tile_free, TILE0["attgate"] + h + 1)
                    ga = gate_a[:, h, b * P:(b + 1) * P]
                    v.tensor_tensor(ga, sum_bank[i % 2][:, 0:P], ga, ALU.mult).then_inc(att_ready, 1)
            for h in range(HEADS):
                dve.wait_ge(a_high, h + 1)
                v.tensor_tensor(a_lo[:, h, :], gate_a[:, h, :], a_hi[:, h, :].bitcast(F32), ALU.subtract).then_inc(a_low, 1)

            def spread(col, n_):
                return col.unsqueeze(2).to_broadcast([P, PAIRS, n_])

            dve.wait_ge(bc_loaded, 9 * 16)
            t_b = b_blk[:, 0, :, :, 0:1, :].rearrange("p q a b c -> p (q a b) c")
            for r, op in ((0, ALU.subtract), (1, ALU.add)):
                tt(b_bar[:, r, :, :], b_raw[:, r, :, :], spread(p_(CR), GCH), ALU.mult)
                tt(t_b, b_raw[:, 1 - r, :, :], spread(p_(CI), GCH), ALU.mult)
                tt(b_bar[:, r, :, :], b_bar[:, r, :, :], t_b, op)
            for r in range(2):
                for g in range(2):
                    dst = b_blk[:, r, :, :, g:g + 1, :].rearrange("p q a b c -> p (q a b) c")
                    link(v.tensor_scalar(dst, b_bar[:, r, :, :], cols[:, 4 + g:5 + g], None, ALU.mult))
            par_b = parity[:, :].unsqueeze(1).to_broadcast([P, QUADS, P])
            link(v.tensor_tensor(c_nat[:, 0, :, :], c_nat[:, 0, :, :], par_b, ALU.mult))
            v.tensor_tensor(c_nat[:, 1, :, :], c_nat[:, 1, :, :], par_b, ALU.mult).then_inc(ssm_w_ready, 1)
            dve.wait_ge(ssm_w_turned, 1)
            link(v.tensor_copy(b_w[:, 0, :, :].rearrange("p q n -> p (q n)"), pair_bank[0][:, :]))
            v.tensor_copy(b_w[:, 1, :, :].rearrange("p q n -> p (q n)"), pair_bank[1][:, :]).then_inc(b_w_done, 1)
            link(v.memset(e_base[:, 0, :, 0:1], 1.0))
            link(v.memset(e_base[:, 1, :, 0:1], 0.0))
            for l in range(5):
                n_ = 2 ** l
                er, ei = e_base[:, 0, :, 0:n_], e_base[:, 1, :, 0:n_]
                rr, ri = spread(rotors[l][0], n_), spread(rotors[l][1], n_)
                ta, tb = b_raw[:, 0, :, 0:n_], b_raw[:, 1, :, 0:n_]
                tt(ta, er, rr, ALU.mult)
                tt(tb, ei, ri, ALU.mult)
                tt(e_base[:, 0, :, n_:2 * n_], ta, tb, ALU.subtract)
                tt(ta, er, ri, ALU.mult)
                tt(tb, ei, rr, ALU.mult)
                tt(e_base[:, 1, :, n_:2 * n_], ta, tb, ALU.add)

            def y_of_quad(q):
                dve.wait_ge(ssm_loaded, 3 * 16)
                dve.wait_ge(y_done, 4 * q + 4)
                v.scalar_tensor_tensor(uT[:, q, :], uT[:, q, :], g_cols[:, 36 + q:37 + q], sum_bank[q % 2][:, :],
                                       ALU.mult, ALU.add).then_inc(y_ready, 1)

            def mark(ins):
                count[0] += 1
                ins.then_inc(v_step, 1)
                return count[0]

            def e_start(j):
                return mark(v.tensor_copy(e_tab[:, j % 2, :, 0:E_BASE], e_base[:, :, j, :]))

            def e_products(j, l, ready):
                n_, ri = 2 ** l, rotors[l][1][:, j:j + 1]
                dve.wait_ge(v_step, ready)
                mark(v.tensor_scalar(e_prod[:, 0, 0:n_], e_tab[:, j % 2, 1, 0:n_], ri, None, ALU.mult))
                return mark(v.tensor_scalar(e_prod[:, 1, 0:n_], e_tab[:, j % 2, 0, 0:n_], ri, None, ALU.mult))

            def e_double(j, l, ready):
                n_, rr = 2 ** l, rotors[l][0][:, j:j + 1]
                er, ei = e_tab[:, j % 2, 0, :], e_tab[:, j % 2, 1, :]
                dve.wait_ge(v_step, ready)
                mark(v.scalar_tensor_tensor(er[:, n_:2 * n_], er[:, 0:n_], rr, e_prod[:, 0, 0:n_], ALU.mult, ALU.subtract))
                return mark(v.scalar_tensor_tensor(ei[:, n_:2 * n_], ei[:, 0:n_], rr, e_prod[:, 1, 0:n_], ALU.mult, ALU.add))

            dve.wait_ge(tile_done, TILE0["merge0"])
            e = e_start(0)
            for l in range(5, 9):
                e = e_products(0, l, e)
                e = e_double(0, l, e)
            p0, p1, p2, p3 = prod[:, 0, :], prod[:, 1, :], prod2[:, 0, :], prod2[:, 1, :]
            zr, zi = z_ri[:, 0, :], z_ri[:, 1, :]
            br, bi = pair_bank[0][:, :], pair_bank[1][:, :]
            dve.wait_ge(v_step, e)
            for j in range(PAIRS):
                er, ei = e_tab[:, j % 2, 0, :], e_tab[:, j % 2, 1, :]
                nxt = j + 1 < PAIRS
                dve.wait_ge(bu_done, j + 1)
                v.tensor_tensor(p0, br, er, ALU.mult)
                mark(v.tensor_tensor(p1, bi, ei, ALU.mult))
                v.tensor_tensor(p2, bi, er, ALU.mult)
                v.tensor_tensor(p3, br, ei, ALU.mult).then_inc(bu_used, 1)
                e = e_start(j + 1) if nxt else 0
                dve.wait_ge(bu_used, j + 1)
                mark(v.tensor_tensor(zr, p0, p1, ALU.add))
                a = mark(v.tensor_tensor(zi, p2, p3, ALU.subtract))
                e = e_products(j + 1, 5, e) if nxt else 0
                dve.wait_ge(v_step, a)
                mag = p_(MAG)[:, j:j + 1].to_broadcast([P, SEQ])
                mark(v.tensor_tensor_scan(zr, mag, zr, 0.0, ALU.mult, ALU.add))
                a = mark(v.tensor_tensor_scan(zi, mag, zi, 0.0, ALU.mult, ALU.add))
                e = e_double(j + 1, 5, e) if nxt else 0
                e = e_products(j + 1, 6, e) if nxt else 0
                dve.wait_ge(v_step, a)
                v.tensor_tensor(p0, zr, er, ALU.mult)
                v.tensor_tensor(p1, zi, ei, ALU.mult)
                v.tensor_tensor(p2, zr, ei, ALU.mult)
                a = mark(v.tensor_tensor(p3, zi, er, ALU.mult))
                e = e_double(j + 1, 6, e) if nxt else 0
                dve.wait_ge(v_step, a)
                if j:
                    dve.wait_ge(y_done, j)
                v.tensor_tensor(x_ri[:, 0, :], p0, p1, ALU.subtract)
                v.tensor_tensor(x_ri[:, 1, :], p2, p3, ALU.add).then_inc(x_ready, 1)
                for l in range(7, 9) if nxt else ():
                    e = e_products(j + 1, l, e)
                    e = e_double(j + 1, l, e)
                dve.wait_ge(x_ready, j + 1)
                if j >= 4 and j % 4 == 0:
                    y_of_quad(j // 4 - 1)
                dve.wait_ge(tile_free, TILE0["merge0"] + j + 1)
                v.tensor_tensor(ya[:, j, :], ya[:, j, :], gate[:, j % 2, :], ALU.mult).then_inc(gate_used, 1)
                if nxt:
                    dve.wait_ge(v_step, e)
            y_of_quad(QUADS - 1)

            def split_s(k, ready):
                link(v.tensor_copy(s_hi[:, k, :], uT[:, k, :]))
                v.tensor_tensor(s_lo[:, k, :], uT[:, k, :], s_hi[:, k, :].bitcast(F32), ALU.subtract).then_inc(ready, 1)

            for k in range(QUADS):
                dve.wait_ge(gelu_done, k + 1)
                split_s(k, s_ready)
            dve.wait_ge(tile_free, TILE0["glu"] + 4)
            for k in range(QUADS):
                link(v.tensor_tensor(uT[:, k, :], uT[:, k, :], gate_glu[:, k, :], ALU.mult))
                if k == QUADS - 1:
                    dve.wait_ge(tile_free, TILE0["ssmgate_last"] + 1)
                link(v.tensor_tensor(uT[:, k, :], uT[:, k, :], gate_s[:, k, :], ALU.mult))
                split_s(k, g_ready)
            dve.wait_ge(gate_used, KD)
            for j in range(KD):
                dve.wait_ge(tile_free, TILE0["merge1"] + j + 1)
                g_ = gate[:, j % 2, :]
                link(v.tensor_tensor(g_, g_, yb[:, j, :], ALU.mult))
                v.tensor_tensor(ya[:, j, :], ya[:, j, :], g_, ALU.add).then_inc(gate_used, 1)
            for j in range(KD):
                dve.wait_ge(m_high, j + 1)
                v.tensor_tensor(act_lo[:, j, :], ya[:, j, :], act_hi[:, j, :].bitcast(F32), ALU.subtract).then_inc(m_low, 1)

            def finish(t):
                dve.wait_ge(squares_done, t + 1)
                link(v.reciprocal(small[:, 188 + t:189 + t], small[:, 184 + t:185 + t]))
                v.scalar_tensor_tensor(res[:, t, :], res[:, t, :], small[:, 188 + t:189 + t], g_row[:, :], ALU.mult, ALU.mult
                                       ).then_inc(final_done, 1)

            dve.wait_ge(res_loaded, 16 * TOK)
            dve.wait_ge(gf_loaded, 16)
            for half in range(2):
                for t in range(TOK):
                    for n in range(2):
                        if (t, n) == (TOK - 1, 1):
                            dve.wait_ge(tile_done, TILE0["out"] + 8 * half + 8)
                        else:
                            dve.wait_ge(bank_done, 7 * half + 2 * t + n + 1)
                        part = res[:, t, half * 1024 + n * 512:half * 1024 + n * 512 + 512]
                        v.tensor_tensor(part, banks[2 * t + n][:, :], part, ALU.add).then_inc(bank_taken, 1)
                    if half == 1 and t >= 1:
                        finish(t - 1)
            finish(TOK - 1)


_INS = ["x", "positions", "g_norm", "w_in", "b_merge", "a_re", "a_im", "log_dt", "ssm_b_re", "ssm_b_im", "ssm_c_re",
        "ssm_c_im", "ssm_d", "w_glu", "b_glu", "w_att_out", "w_ssm_out", "w_out", "g_final"]


def kernel(**inputs):
    from concourse import bacc
    from concourse.bass_utils import run_bass_kernel_spmd

    nc = bacc.Bacc("TRN2", target_bir_lowering=False, num_devices=1)
    arrays, args = {}, []
    given = {name: np.ascontiguousarray(inputs[name]) for name in _INS} | constants()
    for name, a in given.items():
        arrays[f"in_{name}"] = a
        args.append(nc.dram_tensor(f"in_{name}", a.shape, mybir.dt.from_np(a.dtype), kind="ExternalInput").ap())
    out = nc.dram_tensor("out_dram", (1, SEQ, D), F32, kind="ExternalOutput").ap()
    hybrid_kernel(nc, *args, out)
    r = run_bass_kernel_spmd(nc, [arrays], core_ids=[0])
    return r.results[0]["out_dram"]
```

```python
from contextlib import ExitStack

import concourse.bass as bass
import numpy as np
from concourse import mybir

F32 = mybir.dt.float32
F32R = mybir.dt.float32r
I32 = mybir.dt.int32
ALU = mybir.AluOpType
ACT = mybir.ActivationFunctionType
AX_X = mybir.AxisListType.X

P = 128
SEQ = 512
D = 2048
TOK = SEQ // P
KD = D // P
EPS = 1e-6

HEADS, KV_HEADS, HD = 8, 2, 128
ATT_W, KV_W = HEADS * HD, KV_HEADS * HD
IDX_HEADS, IDX_DIM, TOPK, CHUNK = 16, 64, 128, 64
THETA = 500000.0
GROUPS, GCH, STATE = 32, 16, 64
SSM_W = GROUPS * GCH
PAIRS = GROUPS // 2
QUADS = PAIRS // 4

WIDTHS = (ATT_W, KV_W, KV_W, ATT_W, IDX_HEADS * IDX_DIM, IDX_DIM, IDX_HEADS, SSM_W, SSM_W, 2 * D)
COL_Q, COL_K, COL_V, COL_AG, COL_QI, COL_KI, COL_WI, COL_U, COL_SG, COL_MERGE = (
    int(c) for c in np.cumsum((0,) + WIDTHS[:-1]))

V_COLS = 1344
UNIT = 2048
REPLACED = -3.4e38
MASKED = -3.0e38
TOOK_BELOW = -3.2e38
ROUND = 1.5 * 2.0 ** 23
PI = float(np.pi)
INV_2PI = float(1.0 / (2.0 * np.pi))
E_BASE = 32

SEGMENTS = [("kidx", 1, 1), ("qidx", 8, 1), ("k", 2, 1), ("v", 2, 1), ("q", 8, 1), ("attgate", 8, 1), ("u", 4, 1),
            ("attout", 8, 2), ("merge0", 16, 1), ("ssmgate", 4, 1), ("glu", 1, 4), ("merge1_first", 2, 1),
            ("ssmout", 4, 4), ("merge1", 14, 1), ("out", 16, 1)]
EARLY = 2
PER_UNIT = {name: k for name, _, k in SEGMENTS}
UNIT0, TILE0 = {}, {}
_u = _t = 0
for _name, _n, _k in SEGMENTS:
    UNIT0[_name], TILE0[_name] = _u, _t
    _u, _t = _u + _n, _t + _n * _k

ITEMS_PER_UNIT = 4
ATT_STEPS = {("attgate", 6): range(0, 5), ("attgate", 7): range(5, 10),
             ("u", 0): range(10, 18), ("u", 1): range(18, 27), ("u", 2): range(27, 35)}


def split12(x):
    parts = []
    for _ in range(3):
        m, e = np.frexp(x)
        part = float(np.ldexp(np.round(m * 4096.0), e - 12))
        parts.append(part)
        x = x - part
    return parts


def constants():
    row = np.arange(P)
    freq = np.zeros((P, 6), np.float32)
    half = HD // 8
    inv = np.exp(np.float32(-np.log(THETA)) * np.arange(half, dtype=np.float32) * np.float32(2.0 / (2 * half)))
    freq[:, 0] = np.where(row < 2 * half, inv[row % half], 0)
    freq[:, 1] = np.where(row < half, -1, np.where(row < 2 * half, 1, 0))
    half = IDX_DIM // 8
    inv = np.exp(np.float32(-np.log(THETA)) * np.arange(half, dtype=np.float32) * np.float32(2.0 / (2 * half)))
    r = row % IDX_DIM
    freq[:, 2] = np.where(r < 2 * half, inv[r % half], 0)
    freq[:, 3] = np.where(r < half, -1, np.where(r < 2 * half, 1, 0))
    freq[:, 4] = row < STATE
    freq[:, 5] = row >= STATE
    parity = (row[:, None] // GCH) % 2 == (row[None, :] // STATE)
    return {"c_cols": freq, "c_ident": np.eye(P, dtype=np.float32), "c_parity": parity.astype(np.float32)}


def hybrid_kernel(nc, x, positions, g_norm, w_in, b_merge, a_re, a_im, log_dt, b_re, b_im, c_re, c_im, d_skip,
                  w_glu, b_glu, w_att_out, w_ssm_out, w_out, g_final, c_cols, c_ident, c_parity, out):
    w_in_v = w_in[0].rearrange("(k p) n -> p k n", p=P)
    w_att_v = w_att_out[0].rearrange("(k p) n -> p k n", p=P)
    w_ssm_v = w_ssm_out[0].rearrange("(k p) n -> p k n", p=P)
    w_glu_v = w_glu[0].rearrange("(k p) n -> p k n", p=P)
    w_out_v = w_out[0].rearrange("(k p) n -> p k n", p=P)
    x_v = x[0].rearrange("(t p) d -> t p d", p=P)
    out_v = out[0].rearrange("(t p) d -> t p d", p=P)

    with ExitStack() as ctx:
        base = -(-nc.sbuf_base // 32) * 32
        cursor = [base]

        def region(size):
            at = cursor[0]
            cursor[0] += size
            return at

        def at(name, offset, shape, dt=F32):
            return nc.alloc_sbuf_tensor_at(name, [P] + shape, dt, offset=offset)

        KB = 1024
        act_hi = at("act_hi", region(32 * KB), [KD, SEQ], F32R)
        act_lo = at("act_lo", region(32 * KB), [KD, SEQ], F32R)
        w_raw = at("w_raw", region(16 * KB), [2, UNIT])
        w_hi = at("w_hi", region(16 * KB), [2, UNIT], F32R)
        w_lo = at("w_lo", region(16 * KB), [2, UNIT], F32R)
        uT = at("uT", region(8 * KB), [QUADS, SEQ])
        ident = at("ident", region(KB // 2), [P])
        cols = at("cols", region(32), [6])
        g_cols = at("g_cols", region(160), [40])
        small = at("small", region(KB), [256])

        par = at("par", region(18 * 64), [18, PAIRS])
        rot = at("rot", region(KB), [2, 8, PAIRS])

        r1 = region(32 * KB)
        o = [r1]

        def take(name, shape, dt=F32):
            size = int(np.prod(shape)) * 4
            here = o[0]
            o[0] += size
            return at(name, here, shape, dt)

        rot_idx = take("rot_idx", [2, SEQ])
        rot_head = take("rot_head", [2, SEQ])
        kidx_hi = take("kidx_hi", [SEQ], F32R)
        kT = take("kT", [KV_HEADS, SEQ])
        w_idxT = at("w_idxT", o[0], [SEQ])
        v_tok = take("v_tok", [TOK, KV_W])
        tmp = take("tmp", [SEQ])
        kidx_lo = take("kidx_lo", [SEQ], F32R)
        w_idx = take("w_idx", [TOK, IDX_HEADS])
        relu = at("relu", o[0], [2, SEQ])
        k_raw = at("k_raw", o[0], [SEQ])
        pT = take("pT", [2, SEQ])
        vT = take("vT", [KV_HEADS, SEQ])
        pos_i = at("pos_i", o[0] - 4 * KB, [SEQ], I32)
        pos_f = at("pos_f", o[0] - 2 * KB, [SEQ])
        assert o[0] <= r1 + 32 * KB
        ya = at("ya", r1, [KD, SEQ])

        r2 = region(32 * KB)
        xt = at("xt", r2, [TOK, D])
        xg = at("xg", r1, [2, D])
        q_even = at("q_even", r2 + 16 * KB, [8, SEQ - P], F32R)
        q_odd_a = at("q_odd_a", r2 + 28 * KB, [2, SEQ - P], F32R)
        qT = at("qT", r2, [HEADS, SEQ])
        gate_a = at("gate_a", r2 + 16 * KB, [HEADS, SEQ])
        a_hi = at("a_hi", r2, [HEADS, SEQ], F32R)
        o[0] = r2 + 16 * KB
        b_raw = take("b_raw", [2, PAIRS, GCH])
        b_bar = at("b_bar", o[0], [2, PAIRS, GCH])
        b_lo = [None, at("b_lo1", o[0] - 2 * KB, [QUADS, P], F32R)]
        b_hi = take("b_hi", [2, QUADS, P], F32R)
        c_w = at("c_w", o[0], [2, QUADS, P])
        b_blk = take("b_blk", [2, QUADS, 4, 2, GCH])
        e_base = at("e_base", o[0], [2, PAIRS, E_BASE])
        c_nat = take("c_nat", [2, QUADS, P])
        parity = take("parity", [P])
        assert o[0] <= r2 + 32 * KB
        o[0] = r2
        z_ri = take("z_ri", [2, SEQ])
        prod = take("prod", [2, SEQ])
        x_ri = take("x_ri", [2, SEQ])
        u_hi, u_lo = take("u_hi", [SEQ], F32R), take("u_lo", [SEQ], F32R)
        assert o[0] <= r2 + 16 * KB
        gate_s = at("gate_s", r2, [QUADS, SEQ])
        gate_glu = at("gate_glu", r2 + 8 * KB, [QUADS, SEQ])
        yb = at("yb", r2, [KD, SEQ])
        res = at("res", r2, [TOK, D])
        rest = at("rest", r1 + 24 * KB, [D - V_COLS])
        g_last = at("g_last", r1 + 16 * KB, [D])

        r3 = region(16 * KB)
        g_row = at("g_row", r3, [D])
        square = at("square", r3 + 8 * KB, [D])
        o[0] = r3
        score = take("score", [P * 9])
        bias0 = take("bias0", [P])
        q_odd_b = at("q_odd_b", o[0], [6, SEQ - P], F32R)
        assert o[0] + 9 * KB <= r3 + 16 * KB
        probs = take("probs", [3, SEQ])
        assert o[0] <= r3 + 16 * KB
        a_lo = at("a_lo", r3, [HEADS, SEQ], F32R)
        s_hi = at("s_hi", r3, [QUADS, SEQ], F32R)
        s_lo = at("s_lo", r3 + 8 * KB, [QUADS, SEQ], F32R)
        o[0] = r3
        e_tab = take("e_tab", [2, 2, SEQ])
        prod2 = take("prod2", [2, SEQ])
        e_prod = take("e_prod", [2, SEQ // 2])
        b_lo[0] = take("b_lo0", [QUADS, P], F32R)
        r4 = region(4 * KB)
        gate = at("gate", r4, [2, SEQ])
        ang = at("ang", r4, [2, SEQ])
        q_raw = at("q_raw", r4, [2, SEQ])
        assert cursor[0] <= nc.sbuf_usable_end, cursor[0]
        nc.alloc_sbuf_tensor("arena", [P, (cursor[0] - nc.sbuf_base) // 4], F32)

        banks = [ctx.enter_context(nc.psum_tensor(f"bank{i}", [P, 512], F32)) for i in range(8)]
        stream_bank, pair_bank, turn_bank, sum_bank = banks[0:2], banks[2:4], banks[4:6], banks[6:8]

        def sem(name):
            return ctx.enter_context(nc.semaphore(name))

        raw_loaded = [sem("raw_loaded0"), sem("raw_loaded1")]
        high_done, split_done = sem("high_done"), sem("split_done")
        slot_claimed = sem("slot_claimed")
        tile_done, tile_free = sem("tile_done"), sem("tile_free")
        x_loaded = [sem(f"x_loaded{t}") for t in range(TOK)]
        ident_loaded, consts_loaded, g_loaded, ssm_loaded = (sem(n) for n in ("ident_loaded", "consts_loaded", "g_loaded", "ssm_loaded"))
        rstd_ready = sem("rstd_ready")
        rms_done, h_turned, h_high, h_low = (sem(n) for n in ("rms_done", "h_turned", "h_high", "h_low"))
        h_ready = sem("h_ready")
        v_step, a_step = sem("v_step"), sem("a_step")
        ang_ready, table_done = sem("ang_ready"), sem("table_done")
        kidx_ready = sem("kidx_ready")
        qidx_ready, logit_done, relu_done, acc_done = (sem(n) for n in ("qidx_ready", "logit_done", "relu_done", "acc_done"))
        wv_turned, wv_ready = sem("wv_turned"), sem("wv_ready")
        qk_ready = sem("qk_ready")
        scores_done, masked, exp_done, probs_ready, p_turned, pT_ready, pv_done, att_ready = (
            sem(n) for n in ("scores_done", "masked", "exp_done", "probs_ready", "p_turned", "pT_ready", "pv_done", "att_ready"))
        a_high, a_low = sem("a_high"), sem("a_low")
        par_go, par_done = sem("par_go"), sem("par_done")
        ssm_w_ready, ssm_w_turned, c_w_done = sem("ssm_w_ready"), sem("ssm_w_turned"), sem("c_w_done")
        bu_done, bu_used, x_ready, y_done, y_ready, gelu_done = (
            sem(n) for n in ("bu_done", "bu_used", "x_ready", "y_done", "y_ready", "gelu_done"))
        gate_used = sem("gate_used")
        s_ready, g_ready, m_high, m_low = sem("s_ready"), sem("g_ready"), sem("m_high"), sem("m_low")
        bank_taken, squares_done, final_done, stored = (sem(n) for n in ("bank_taken", "squares_done", "final_done", "stored"))
        scale_ready, rest_ready, final_rest_done = sem("scale_ready"), sem("rest_ready"), sem("final_rest_done")
        xg_ready = sem("xg_ready")
        res_loaded, gf_loaded, bank_done = sem("res_loaded"), sem("gf_loaded"), sem("bank_done")
        kidx_raw, nmax_ready, bc_loaded, par_loaded = (sem(n) for n in ("kidx_raw", "nmax_ready", "bc_loaded", "par_loaded"))
        b_split, u_high, u_low, e_grown, e_scaled = (sem(n) for n in ("b_split", "u_high", "u_low", "e_grown", "e_scaled"))

        block = ctx.enter_context(nc.Block())

        def tiles_through(u):
            for name, n, k in reversed(SEGMENTS):
                if u >= UNIT0[name]:
                    return TILE0[name] + (u - UNIT0[name] + 1) * k
            return 0

        def q_parts(h):
            i = h // 2
            return q_even[:, i, :] if h % 2 == 0 else q_odd_a[:, i, :] if i < 2 else q_odd_b[:, i - 2, :]

        def merge1_tile(j):
            return TILE0["merge1_first"] + j if j < EARLY else TILE0["merge1"] + j - EARLY

        def unit_loop(eng, name, body):
            n = dict((s, c) for s, c, _ in SEGMENTS)[name]
            u0 = UNIT0[name]
            if n < 4:
                for i in range(n):
                    body(u0 + i, (u0 + i) % 2, i)
                return
            with eng.Fori(0, n // 2) as i:
                for half in range(2):
                    body(u0 + half + 2 * i, (u0 + half) % 2, 2 * i + half)

        @block.sync
        def _(sp):
            def raw(slot, k):
                return w_raw[:, slot, :].rearrange("p (k n) -> p k n", k=k)

            def loads(name, source, k):
                def body(u, slot, i):
                    sp.wait_ge(split_done, u - 1)
                    sp.dma_start(raw(slot, k), source(i)).then_inc(raw_loaded[slot], 16)
                unit_loop(sp, name, body)

            def w_in_cols(col):
                return lambda i: w_in_v[:, :, bass.ds(col + P * i, P)]

            sp.dma_start(xt[:, 0, :], x_v[0]).then_inc(x_loaded[0], 16)
            sp.dma_start(ident[:, :], c_ident).then_inc(ident_loaded, 16)
            sp.dma_start(g_row[:, :], g_norm.to_broadcast([P, D])).then_inc(g_loaded, 16)
            for t in range(1, TOK):
                sp.dma_start(xt[:, t, :], x_v[t]).then_inc(x_loaded[t], 16)
            n0 = IDX_DIM + IDX_HEADS
            sp.dma_start(w_raw[:, 0, 0:KD * n0].rearrange("p (k n) -> p k n", k=KD),
                         w_in_v[:, :, COL_KI:COL_KI + n0]).then_inc(raw_loaded[0], 16)
            for dst, src in ((cols[:, :], c_cols), (pos_i[:, :], positions.to_broadcast([P, SEQ]))):
                sp.dma_start(dst, src).then_inc(consts_loaded, 16)
            sp.dma_start(raw(1, KD), w_in_v[:, :, COL_QI:COL_QI + P]).then_inc(raw_loaded[1], 16)
            sp.wait_ge(split_done, 1)
            sp.dma_start(raw(0, KD), w_in_v[:, :, COL_QI + P:COL_QI + 2 * P]).then_inc(raw_loaded[0], 16)
            with sp.Fori(1, 4) as i:
                for half in range(2):
                    sp.wait_ge(split_done, 2 * i + half)
                    sp.dma_start(raw((1 + half) % 2, KD), w_in_v[:, :, bass.ds(2 * P * i + (COL_QI + half * P), P)]
                                 ).then_inc(raw_loaded[(1 + half) % 2], 16)
            with nc.allow_non_contiguous_dma(reason="one column per feature tile"):
                sp.dma_start(g_cols[:, 0:32], b_merge[0].rearrange("(c p) -> p c", p=P)).then_inc(ssm_loaded, 16)
                sp.dma_start(g_cols[:, 32:36], b_glu[0].rearrange("(c p) -> p c", p=P)).then_inc(ssm_loaded, 16)
                sp.dma_start(g_cols[:, 36:40], d_skip[0].rearrange("(q g) c -> (g c) q", q=QUADS)).then_inc(ssm_loaded, 16)
            loads("k", w_in_cols(COL_K), KD)
            loads("v", w_in_cols(COL_V), KD)
            loads("q", w_in_cols(COL_Q), KD)
            loads("attgate", w_in_cols(COL_AG), KD)
            loads("u", w_in_cols(COL_U), KD)
            loads("attout", lambda i: w_att_v[:, :, bass.ds(2 * P * i, 2 * P)], 8)
            loads("merge0", w_in_cols(COL_MERGE), KD)
            loads("ssmgate", w_in_cols(COL_SG), KD)
            loads("glu", lambda i: w_glu_v, 4)
            loads("merge1_first", w_in_cols(COL_MERGE + D), KD)
            loads("ssmout", lambda i: w_ssm_v[:, :, bass.ds(SSM_W * i, SSM_W)], 4)
            loads("merge1", w_in_cols(COL_MERGE + D + EARLY * P), KD)
            for half in range(2):
                with sp.Fori(0, 4) as i:
                    for p in range(2):
                        slot = (UNIT0["out"] + p) % 2
                        sp.wait_ge(split_done, 2 * i + (UNIT0["out"] + 8 * half + p - 1))
                        sp.dma_start(raw(slot, 2), w_out_v[:, bass.ds(4 * i + 2 * p, 2), half * 1024:half * 1024 + 1024]
                                     ).then_inc(raw_loaded[slot], 16)
                if half == 0:
                    sp.wait_ge(gate_used, 2 * KD)
                    for t in range(TOK):
                        sp.dma_start(res[:, t, :], x_v[t]).then_inc(res_loaded, 16)
                    sp.wait_ge(m_low, KD)
                    sp.dma_start(g_last[:, :], g_final.rearrange("(a d) -> a d", a=1).to_broadcast([P, D])
                                 ).then_inc(gf_loaded, 16)
            for t in range(TOK):
                sp.wait_ge(final_done, t + 1)
                sp.dma_start(out_v[t][:, 0:V_COLS], res[:, t, 0:V_COLS]).then_inc(stored, 16)
                sp.wait_ge(final_rest_done, t + 1)
                sp.dma_start(out_v[t][:, V_COLS:D], res[:, t, V_COLS:D]).then_inc(stored, 16)
            sp.wait_ge(stored, 2 * 16 * TOK)

        @block.gpsimd
        def _(pool):
            pool.wait_ge(g_loaded, 16)
            for i, t in enumerate((1, 2)):
                pool.wait_ge(x_loaded[t], 16)
                pool.tensor_tensor(xg[:, i, :], xt[:, t, :], g_row[:, :], ALU.mult).then_inc(xg_ready, 1)

            def split(slot, u, n_el=UNIT):
                pool.tensor_scalar(w_hi[:, slot, 0:n_el], w_raw[:, slot, 0:n_el], 1.0, 1.0, ALU.mult, ALU.mult
                                   ).then_inc(high_done, 1)
                pool.wait_ge(high_done, u + 1)
                pool.tensor_tensor(w_lo[:, slot, 0:n_el], w_raw[:, slot, 0:n_el], w_hi[:, slot, 0:n_el].bitcast(F32),
                                   ALU.subtract).then_inc(split_done, 1)

            def gate_y_a(j, slot):
                pool.wait_ge(tile_free, j + (TILE0["merge0"] + 1))
                if not isinstance(j, int):
                    pool.sem_inc(slot_claimed, 1)
                here = ya[:, bass.ds(j, 1), :].rearrange("p a n -> p (a n)")
                pool.tensor_tensor(here, here, gate[:, slot, :], ALU.mult).then_inc(gate_used, 1)

            for name, n, k in SEGMENTS:
                u0 = UNIT0[name]
                for u in range(u0, u0 + (n if n < 4 else 2)):
                    pool.wait_ge(raw_loaded[u % 2], 16 * (u // 2 + 1))
                    if u >= 2:
                        pool.wait_ge(tile_done, tiles_through(u - 2))
                    split(u % 2, u, KD * (IDX_DIM + IDX_HEADS) if name == "kidx" else UNIT)
                    if name == "ssmgate":
                        gate_y_a(KD - 2 + u - u0, (u - u0) % 2)
                if n >= 4:
                    with pool.Fori(1, n // 2) as i:
                        for half in range(2):
                            slot = (u0 + half) % 2
                            pool.wait_ge(raw_loaded[slot], 16 * i + 16 * ((u0 + half) // 2 + 1))
                            pool.wait_ge(tile_done, 2 * k * i + (TILE0[name] + (half - 1) * k))
                            pool.sem_inc(slot_claimed, 1)
                            split(slot, 2 * i + (u0 + half))
                            if name == "merge0":
                                gate_y_a(2 * i + (half - 2), half)
            pool.wait_ge(gf_loaded, 16)
            for t in range(TOK):
                pool.wait_ge(bank_taken, 8 + 2 * t + 2)
                if t:
                    pool.wait_ge(final_rest_done, t)
                pool.tensor_tensor(rest[:, :], res[:, t, V_COLS:D], g_last[:, V_COLS:D], ALU.mult).then_inc(rest_ready, 1)

        @block.tensor
        def _(pe):
            def product_high_first(out_ap, terms, x_hi, x_lo):
                for j, (wh, wl, k) in enumerate(terms):
                    nc.tensor.matmul(out_ap, wh, x_hi[k], start=(j == 0), stop=False)
                    nc.tensor.matmul(out_ap, wl, x_hi[k], start=False, stop=False)
                pe.wait_ge(h_low, 16)
                for wh, wl, k in terms:
                    last = nc.tensor.matmul(out_ap, wh, x_lo[k], start=False, stop=(k == terms[-1][2]))
                return last

            def product(out_ap, terms, x_hi, x_lo, between):
                n = len(terms)
                for j, (wh, wl, k) in enumerate(terms):
                    nc.tensor.matmul(out_ap, wh, x_hi[k], start=(j == 0), stop=False)
                    nc.tensor.matmul(out_ap, wh, x_lo[k], start=False, stop=False)
                    last = nc.tensor.matmul(out_ap, wl, x_hi[k], start=False, stop=(j == n - 1))
                    if between and j < n - 1:
                        between(j)
                return last

            h_hi = [act_hi[:, k, :] for k in range(KD)]
            h_lo = [act_lo[:, k, :] for k in range(KD)]

            def project(name, x_hi, x_lo, k_n):
                per = dict((s, c) for s, _, c in SEGMENTS)[name]
                n_el = per * P

                def body(u, slot, i, between=None):
                    pe.wait_ge(split_done, u + 1)
                    for m in range(per):
                        t = (i * per) + (TILE0[name] + m)
                        parity = (TILE0[name] + (per * ((slot - UNIT0[name]) % 2)) + m) % 2
                        if not (isinstance(t, int) and t < 2):
                            pe.wait_ge(tile_free, t - 1)
                        terms = [(w_hi[:, slot, k * n_el + m * P:k * n_el + (m + 1) * P],
                                  w_lo[:, slot, k * n_el + m * P:k * n_el + (m + 1) * P], k) for k in range(k_n)]
                        out_ap = stream_bank[parity][:, 0:x_hi[0].shape[-1]]
                        product(out_ap, terms, x_hi, x_lo, between).then_inc(tile_done, 1)
                return body

            pe.wait_ge(ident_loaded, 16)
            for t in range(TOK):
                pe.wait_ge(h_ready, t + 1)
                for kq in range(4):
                    n = 4 * t + kq
                    if n >= 8:
                        pe.wait_ge(h_low, n - 7)
                    for j in range(4):
                        k = 4 * kq + j
                        last = nc.tensor.transpose(banks[n % 8][:, j * P:(j + 1) * P], xt[:, t, k * P:(k + 1) * P], ident[:, :])
                    last.then_inc(h_turned, 1)
            pe.wait_ge(h_high, 16)
            pe.wait_ge(h_low, 9)
            pe.wait_ge(split_done, 1)
            width = IDX_DIM + IDX_HEADS
            product_high_first(stream_bank[0][0:width, :],
                               [(w_hi[:, 0, k * width:(k + 1) * width], w_lo[:, 0, k * width:(k + 1) * width], k)
                                for k in range(KD)], h_hi, h_lo).then_inc(tile_done, 1)
            late_hi = [act_hi[:, k, P:SEQ] for k in range(KD)]
            late_lo = [act_lo[:, k, P:SEQ] for k in range(KD)]
            qi = project("qidx", late_hi, late_lo, KD)
            qi(1, 1, 0)
            pe.wait_ge(tile_free, 1)
            for t in range(TOK):
                last = nc.tensor.transpose(turn_bank[0][:, IDX_HEADS * t:IDX_HEADS * (t + 1)],
                                           w_idxT[IDX_DIM:IDX_DIM + IDX_HEADS, t * P:(t + 1) * P],
                                           ident[IDX_DIM:IDX_DIM + IDX_HEADS, IDX_DIM:IDX_DIM + IDX_HEADS])
            last.then_inc(wv_turned, 1)
            qi(2, 0, 1)
            with pe.Fori(1, 4) as i:
                qi(2 * i + 1, 1, 2 * i)
                qi(2 * i + 2, 0, 2 * i + 1)

            idx_items = [(b, h) for b in range(1, TOK) for h in range(IDX_HEADS)]

            def indexer_item(n):
                b, h = idx_items[n]
                if n == 0:
                    pe.wait_ge(kidx_ready, 2)
                if b == 1 and h % 2 == 0:
                    pe.wait_ge(qidx_ready, h // 2 + 1)
                if n >= 2:
                    pe.wait_ge(relu_done, n - 1)
                rows = slice(IDX_DIM * (h % 2), IDX_DIM * (h % 2) + IDX_DIM)
                q, keys = q_parts(h)[:, (b - 1) * P:b * P], slice(0, (b + 1) * P)
                nc.tensor.matmul(pair_bank[n % 2][:, keys], q, kidx_hi[:, keys], start=True, stop=False)
                nc.tensor.matmul(pair_bank[n % 2][:, keys], q[rows], kidx_lo[rows, keys], start=False, stop=True
                                 ).then_inc(logit_done, 1)

            done = 0
            for name, count in (("k", 2), ("v", 2), ("q", 8)):
                unit = project(name, h_hi, h_lo, KD)
                for i in range(count):
                    first = ITEMS_PER_UNIT * done
                    unit(UNIT0[name] + i, (UNIT0[name] + i) % 2, i,
                         lambda k: indexer_item(first + k // 4) if k % 4 == 2 else None)
                    done += 1
                    if (name, i) == ("q", 0):
                        pe.wait_ge(wv_ready, 1)
                        pe.wait_ge(tile_free, TILE0["v"] + KV_HEADS)
                        for kv in range(KV_HEADS):
                            for t in range(TOK):
                                last = nc.tensor.transpose(turn_bank[kv][:, t * P:(t + 1) * P], vT[:, kv, t * P:(t + 1) * P],
                                                           ident[:, :])
                        last.then_inc(wv_turned, 1)

            items = [(b, h) for b in range(TOK) for h in range(HEADS)]

            def attention_step(s):
                if s == 0:
                    pe.wait_ge(qk_ready, HEADS + KV_HEADS)
                    pe.wait_ge(wv_ready, 2)
                if s < len(items):
                    b, h = items[s]
                    if s >= 2:
                        pe.wait_ge(masked, s - 1)
                    nc.tensor.matmul(pair_bank[s % 2][:, 0:(b + 1) * P], qT[:, h, b * P:(b + 1) * P],
                                     kT[:, h // 4, 0:(b + 1) * P], start=True, stop=True).then_inc(scores_done, 1)
                if 2 <= s < len(items) + 2:
                    i = s - 2
                    b, h = items[i]
                    pe.wait_ge(probs_ready, i + 1)
                    if i >= 2:
                        pe.wait_ge(pT_ready, i - 1)
                    for k in range(b + 1):
                        last = nc.tensor.transpose(turn_bank[i % 2][:, k * P:(k + 1) * P], probs[:, i % 3, k * P:(k + 1) * P],
                                                   ident[:, :])
                    last.then_inc(p_turned, 1)
                if s >= 3:
                    i = s - 3
                    b, h = items[i]
                    pe.wait_ge(pT_ready, i + 1)
                    if i >= 2:
                        pe.wait_ge(att_ready, i - 1)
                    for k in range(b + 1):
                        last = nc.tensor.matmul(sum_bank[i % 2][:, 0:P], v_tok[:, k, (h // 4) * HD:(h // 4 + 1) * HD],
                                                pT[:, i % 2, k * P:(k + 1) * P], start=(k == 0), stop=(k == b))
                    last.then_inc(pv_done, 1)

            attgate = project("attgate", h_hi, h_lo, KD)
            with pe.Fori(0, 3) as i:
                for half in range(2):
                    attgate(2 * i + (UNIT0["attgate"] + half), (UNIT0["attgate"] + half) % 2, 2 * i + half)
            for name, i in (("attgate", 6), ("attgate", 7), ("u", 0), ("u", 1), ("u", 2), ("u", 3)):
                steps = ATT_STEPS.get((name, i), range(0))
                behind = {(KD - 1) * (n + 1) // len(steps) - 1: s for n, s in enumerate(steps)}
                project(name, h_hi, h_lo, KD)(UNIT0[name] + i, (UNIT0[name] + i) % 2, i,
                                              lambda k: attention_step(behind[k]) if k in behind else None)

            pe.wait_ge(a_low, HEADS)
            attout = project("attout", [a_hi[:, k, :] for k in range(8)], [a_lo[:, k, :] for k in range(8)], 8)
            u0 = UNIT0["attout"]
            with pe.Fori(0, 3) as i:
                for half in range(2):
                    attout(2 * i + (u0 + half), (u0 + half) % 2, 2 * i + half)

            pe.wait_ge(ssm_w_ready, 1)
            for r in range(2):
                for q in range(QUADS):
                    nc.tensor.transpose(pair_bank[r][:, q * P:(q + 1) * P],
                                        b_blk[:, r, q, :, :, :].rearrange("p a b c -> p (a b c)"), ident[:, :])
                    last = nc.tensor.transpose(turn_bank[r][:, q * P:(q + 1) * P], c_nat[:, r, q, :], ident[:, :])
            last.then_inc(ssm_w_turned, 1)
            for i in (6, 7):
                attout(u0 + i, (u0 + i) % 2, i)


            def y_of(j):
                q, jj = j // 4, j % 4
                pe.wait_ge(x_ready, j + 1)
                if q >= 2 and jj == 0:
                    pe.wait_ge(y_ready, q - 1)
                out_ap = sum_bank[q % 2][32 * jj:32 * jj + 32, :]
                nc.tensor.matmul(out_ap, c_w[:, 0, q, 32 * jj:32 * jj + 32], x_ri[:, 0, :], start=True, stop=False)
                nc.tensor.matmul(out_ap, c_w[:, 1, q, 32 * jj:32 * jj + 32], x_ri[:, 1, :], start=False, stop=True
                                 ).then_inc(y_done, 1)

            def bu_of(j):
                q, rows = j // 4, slice(32 * (j % 4), 32 * (j % 4) + 32)
                if j == 0:
                    pe.wait_ge(b_split, 2)
                if j % 4 == 0:
                    pe.wait_ge(u_low, q + 1)
                if j >= 1:
                    pe.wait_ge(bu_used, j)
                for r in range(2):
                    out_ap = pair_bank[r][:, :]
                    nc.tensor.matmul(out_ap, b_hi[rows, r, q, :], u_hi[rows, :], start=True, stop=False)
                    nc.tensor.matmul(out_ap, b_hi[rows, r, q, :], u_lo[rows, :], start=False, stop=False)
                    last = nc.tensor.matmul(out_ap, b_lo[r][rows, q, :], u_hi[rows, :], start=False, stop=True)
                last.then_inc(bu_done, 1)

            for n in range(PAIRS + QUADS):
                name, i = ("merge0", n) if n < PAIRS else ("ssmgate", n - PAIRS)
                if 1 <= n <= PAIRS:
                    bu_of(n - 1)
                if n == 2:
                    pe.wait_ge(c_w_done, 1)
                project(name, h_hi, h_lo, KD)(UNIT0[name] + i, (UNIT0[name] + i) % 2, i,
                                              lambda k: y_of(n - 2) if k == KD // 2 and 2 <= n <= PAIRS + 1 else None)
            sh, sl = [s_hi[:, k, :] for k in range(4)], [s_lo[:, k, :] for k in range(4)]
            pe.wait_ge(s_ready, 4)
            unit_loop(pe, "glu", project("glu", sh, sl, 4))
            unit_loop(pe, "merge1_first", project("merge1_first", h_hi, h_lo, KD))
            pe.wait_ge(g_ready, 4)
            unit_loop(pe, "ssmout", project("ssmout", sh, sl, 4))
            unit_loop(pe, "merge1", project("merge1", h_hi, h_lo, KD))

            for half in range(2):
                for c in range(8):
                    u = UNIT0["out"] + 8 * half + c
                    pe.wait_ge(split_done, u + 1)
                    if half == 0:
                        pe.wait_ge(m_low, 2 * c + 2)
                    ks = (2 * c, 2 * c + 1)
                    steps = [(k, t, n) for k in ks for t in (1, 2, 3, 0) for n in range(2)]
                    if c == 7:
                        steps = [(k, t, n) for t in range(TOK) for n in range(2) for k in ks]
                    for k, t, n in steps:
                        if half == 0 and (k, t, n) == (0, 0, 0):
                            pe.wait_ge(tile_free, TILE0["out"])
                        if half == 1 and k == 0:
                            pe.wait_ge(bank_taken, 2 * t + n + 1)
                        out_ap = banks[2 * t + n][:, :]
                        m_hi, m_lo = (s_hi, s_lo) if k < QUADS else (act_hi, act_lo)
                        mh, ml = m_hi[:, k, t * P:(t + 1) * P], m_lo[:, k, t * P:(t + 1) * P]
                        slot = u % 2
                        w = slice(k % 2 * 1024 + n * 512, k % 2 * 1024 + n * 512 + 512)
                        nc.tensor.matmul(out_ap, mh, w_hi[:, slot, w], start=(k == 0), stop=False)
                        nc.tensor.matmul(out_ap, mh, w_lo[:, slot, w], start=False, stop=False)
                        last = nc.tensor.matmul(out_ap, ml, w_hi[:, slot, w], start=False, stop=(k == KD - 1))
                        if k == KD - 1 and (t, n) != (TOK - 1, 1):
                            last.then_inc(bank_done, 1)
                    last.then_inc(tile_done, 1)

        @block.scalar
        def _(act):
            count = [0]

            def link(ins):
                count[0] += 1
                ins.then_inc(a_step, 1)
                act.wait_ge(a_step, count[0])

            def copy_tile(t, dst, src, func=ACT.Copy, **kw):
                act.wait_ge(tile_done, t + 1)
                nc.scalar.activation(dst, src, func, **kw).then_inc(tile_free, 1)

            act.wait_ge(par_go, 1)
            link(nc.scalar.activation(small[:, 252:253], small[:, 250:251], ACT.Sqrt))

            def rms_of(t):
                act.wait_ge(x_loaded[t], 16)
                link(nc.scalar.activation(square[:, :], xt[:, t, :], ACT.Square, accum_out=small[:, t:t + 1]))
                nc.scalar.activation(small[:, 8 + t:9 + t], small[:, t:t + 1], ACT.Sqrt, bias=small[:, 250:251], scale=1.0 / D
                                     ).then_inc(rms_done, 1)

            rms_of(0)
            for t in range(TOK):
                if t + 1 < TOK:
                    rms_of(t + 1)
                for kq in range(4):
                    n = 4 * t + kq
                    act.wait_ge(h_turned, n + 1)
                    nc.scalar.activation(act_hi[:, 4 * kq:4 * kq + 4, t * P:(t + 1) * P],
                                         banks[n % 8][:, :].rearrange("p (k n) -> p k n", k=4), ACT.Copy).then_inc(h_high, 1)
            act.wait_ge(tile_done, 1)
            nc.scalar.activation(k_raw[0:IDX_DIM, :], stream_bank[0][0:IDX_DIM, :], ACT.Copy).then_inc(kidx_raw, 1)
            nc.scalar.activation(w_idxT[IDX_DIM:IDX_DIM + IDX_HEADS, :], stream_bank[0][IDX_DIM:IDX_DIM + IDX_HEADS, :],
                                 ACT.Copy).then_inc(tile_free, 1)
            for w in range(2):
                table = (rot_idx, rot_head)[w]
                act.wait_ge(ang_ready, w + 1)
                nc.scalar.activation(table[:, 1, :], ang[:, 0, :], ACT.Sin, scale=cols[:, 3 - 2 * w:4 - 2 * w]).then_inc(table_done, 1)
                nc.scalar.activation(table[:, 0, :], ang[:, 1, :], ACT.Sin, scale=-1.0, bias=small[:, 251:252]).then_inc(table_done, 1)

            act.wait_ge(table_done, 4)
            copy_tile(1, q_raw[:, 0, 0:SEQ - P], stream_bank[1][:, 0:SEQ - P])
            act.wait_ge(wv_turned, 1)
            nc.scalar.activation(w_idx[:, :, :].rearrange("p t h -> p (t h)"), turn_bank[0][:, 0:TOK * IDX_HEADS], ACT.Copy,
                                 scale=IDX_HEADS ** -0.5).then_inc(wv_ready, 1)
            for i in range(1, 8):
                if i >= 2:
                    act.wait_ge(qidx_ready, i - 1)
                copy_tile(1 + i, q_raw[:, i % 2, 0:SEQ - P], stream_bank[(1 + i) % 2][:, 0:SEQ - P])
            with nc.allow_non_contiguous_dma(reason="one column per pair of groups"):
                for g in range(2):
                    rows = slice(STATE * g, STATE * g + STATE)
                    act.dma_start(par[rows, 0, :], a_re[0].rearrange("(j g) p -> g p j", g=2)[g]).then_inc(par_loaded, 16)
                    act.dma_start(par[rows, 1, :], a_im[0].rearrange("(j g) p -> g p j", g=2)[g]).then_inc(par_loaded, 16)
                    act.dma_start(par[rows, 2, :], log_dt.rearrange("o (j g) -> g o j", g=2)[g].to_broadcast([STATE, PAIRS])
                                  ).then_inc(par_loaded, 16)
            n = 0
            for dst in [kT[:, i, :] for i in range(2)] + [vT[:, i, :] for i in range(2)] + [qT[:, i, :] for i in range(8)]:
                for _ in range(ITEMS_PER_UNIT):
                    b = 1 + n // IDX_HEADS
                    act.wait_ge(logit_done, n + 1)
                    if n >= 2:
                        act.wait_ge(acc_done, n - 1)
                    nc.scalar.activation(relu[:, n % 2, 0:(b + 1) * P], pair_bank[n % 2][:, 0:(b + 1) * P], ACT.Relu,
                                         scale=IDX_DIM ** -0.5).then_inc(relu_done, 1)
                    n += 1
                t = TILE0["k"] + n // ITEMS_PER_UNIT - 1
                copy_tile(t, dst, stream_bank[t % 2][:, :])
                if t == TILE0["q"]:
                    act.wait_ge(wv_turned, 2)
                    for kv in range(KV_HEADS):
                        last = nc.scalar.activation(v_tok[:, :, kv * HD:(kv + 1) * HD],
                                                    turn_bank[kv][:, :].rearrange("p (t d) -> p t d", t=TOK), ACT.Copy)
                    last.then_inc(wv_ready, 1)

            items = [(b, h) for b in range(TOK) for h in range(HEADS)]

            def attention_step(s):
                if s < len(items):
                    b, h = items[s]
                    act.wait_ge(masked, s + 1)
                    act.wait_ge(nmax_ready, s + 1)
                    nc.scalar.activation(probs[:, s % 3, 0:(b + 1) * P], probs[:, s % 3, 0:(b + 1) * P], ACT.Exp,
                                         bias=small[:, 64 + s:65 + s], scale=HD ** -0.5, accum_out=small[:, 96 + s:97 + s]
                                         ).then_inc(exp_done, 1)
                if 2 <= s < len(items) + 2:
                    i = s - 2
                    b, h = items[i]
                    act.wait_ge(p_turned, i + 1)
                    if i >= 2:
                        act.wait_ge(pv_done, i - 1)
                    nc.scalar.activation(pT[:, i % 2, 0:(b + 1) * P], turn_bank[i % 2][:, 0:(b + 1) * P], ACT.Copy
                                         ).then_inc(pT_ready, 1)

            for i in range(HEADS):
                for s in ATT_STEPS.get(("attgate", i), ()):
                    attention_step(s)
                t = TILE0["attgate"] + i
                copy_tile(t, gate_a[:, i, :], stream_bank[t % 2][:, :], ACT.Silu)
                if i == 2:
                    act.wait_ge(par_loaded, 6 * 16)
                    nc.scalar.activation(par[:, 3, :], par[:, 2, :], ACT.Exp).then_inc(par_done, 1)
                    act.wait_ge(par_go, 2)
                    nc.scalar.activation(par[:, 5, :], par[:, 4, :], ACT.Exp).then_inc(par_done, 1)
                    act.wait_ge(par_go, 3)
                    nc.scalar.activation(par[:, 9, :], par[:, 8, :], ACT.Sin).then_inc(par_done, 1)
                    nc.scalar.activation(par[:, 11, :], par[:, 10, :], ACT.Sin, scale=-1.0, bias=small[:, 251:252]
                                         ).then_inc(par_done, 1)
            for i in range(QUADS):
                for s in ATT_STEPS.get(("u", i), ()):
                    attention_step(s)
                if i == QUADS - 1:
                    for h in range(HEADS):
                        act.wait_ge(att_ready, 24 + h + 1)
                        nc.scalar.activation(a_hi[:, h, :], gate_a[:, h, :], ACT.Copy).then_inc(a_high, 1)
                t = TILE0["u"] + i
                copy_tile(t, uT[:, i, :], stream_bank[t % 2][:, :])
            act.wait_ge(a_low, HEADS)
            for r, src in enumerate((b_re, b_im)):
                for g in range(2):
                    act.dma_start(b_raw[STATE * g:STATE * g + STATE, r, :, :],
                                  src[0].rearrange("(j g) p c -> g p j c", g=2)[g]).then_inc(bc_loaded, 16)
            for r, src in enumerate((c_re, c_im)):
                for g in range(2):
                    act.dma_start(c_nat[:, r, :, STATE * g:STATE * g + STATE],
                                  src[0].rearrange("(q g) c p -> (g c) q p", q=QUADS)).then_inc(bc_loaded, 16)
            act.dma_start(parity[:, :], c_parity).then_inc(bc_loaded, 16)
            for i in range(16):
                t = TILE0["attout"] + i
                copy_tile(t, ya[:, i, :], stream_bank[t % 2][:, :])
                if i == 11:
                    act.wait_ge(ssm_w_turned, 1)
                    nc.scalar.activation(c_w[:, 0, :, :].rearrange("p q n -> p (q n)"), turn_bank[0][:, :], ACT.Copy)
                    nc.scalar.activation(c_w[:, 1, :, :].rearrange("p q n -> p (q n)"), turn_bank[1][:, :], ACT.Copy, scale=-1.0
                                         ).then_inc(c_w_done, 1)

            def gelu(q):
                act.wait_ge(y_ready, q + 1)
                nc.scalar.activation(uT[:, q, :], uT[:, q, :], ACT.Gelu_apprx_tanh).then_inc(gelu_done, 1)

            def u_high_part(q):
                nc.scalar.activation(u_hi[:, :], uT[:, q, :], ACT.Copy).then_inc(u_high, 1)

            def e_scale(j):
                for i in range(4):
                    n = E_BASE << i
                    act.wait_ge(e_grown, 5 * j + i + 1)
                    nc.scalar.activation(e_prod[:, :, 0:n], e_tab[:, j % 2, :, 0:n], ACT.Copy, scale=rot[:, 1, 4 + i, j:j + 1]
                                         ).then_inc(e_scaled, 1)

            act.wait_ge(tile_done, TILE0["merge0"])
            u_high_part(0)
            e_scale(0)
            for j in range(KD):
                t = TILE0["merge0"] + j
                if j >= 2:
                    act.wait_ge(gate_used, j - 1)
                if j == 0:
                    act.wait_ge(ssm_loaded, 3 * 16)
                act.wait_ge(tile_done, t + 1)
                nc.scalar.activation(gate[:, j % 2, :], stream_bank[t % 2][:, :], ACT.Sigmoid, bias=g_cols[:, j:j + 1]
                                     ).then_inc(tile_free, 1)
                if j % 4 == 3 and j + 1 < PAIRS:
                    act.wait_ge(bu_done, j + 1)
                    u_high_part((j + 1) // 4)
                if j + 1 < PAIRS:
                    e_scale(j + 1)
                if j >= 6 and (j - 6) % 4 == 0:
                    gelu((j - 6) // 4)
            act.wait_ge(x_ready, PAIRS)
            for i in range(QUADS):
                t = TILE0["ssmgate"] + i
                copy_tile(t, gate_s[:, i, :], stream_bank[t % 2][:, :], ACT.Silu)
                if i == 1:
                    gelu(QUADS - 1)
            for i in range(4):
                t = TILE0["glu"] + i
                copy_tile(t, gate_glu[:, i, :], stream_bank[t % 2][:, :], ACT.Sigmoid, bias=g_cols[:, 32 + i:33 + i])

            def merge1_gate(j):
                act.wait_ge(gate_used, KD + j - 1)
                t = merge1_tile(j)
                copy_tile(t, gate[:, j % 2, :], stream_bank[t % 2][:, :], ACT.Sigmoid, bias=g_cols[:, 16 + j:17 + j])

            def high_of_merge(k):
                act.wait_ge(gate_used, KD + k + 1)
                nc.scalar.activation((s_hi if k < QUADS else act_hi)[:, k, :], ya[:, k, :], ACT.Copy).then_inc(m_high, 1)

            for j in range(EARLY):
                merge1_gate(j)
            with act.Fori(0, KD // 2) as i:
                for half in range(2):
                    t = TILE0["ssmout"] + half
                    copy_tile(2 * i + t, yb[:, bass.ds(2 * i + half, 1), :].rearrange("p a n -> p (a n)"),
                              stream_bank[t % 2][:, :])
            for j in range(EARLY, KD):
                merge1_gate(j)
                if 8 <= j < 8 + QUADS:
                    high_of_merge(j - 8)
            act.wait_ge(tile_done, TILE0["out"])
            for k in range(QUADS, KD):
                high_of_merge(k)
            def scale_rest(t):
                act.wait_ge(rest_ready, t + 1)
                act.wait_ge(scale_ready, t + 1)
                nc.scalar.activation(res[:, t, V_COLS:D], rest[:, :], ACT.Copy, scale=small[:, 188 + t:189 + t]
                                     ).then_inc(final_rest_done, 1)

            n = 0
            for half in range(2):
                for t in range(TOK):
                    for c in range(2):
                        act.wait_ge(bank_taken, n + 1)
                        col = 160 + 4 * t + 2 * half + c
                        lo = half * 1024 + c * 512
                        link(nc.scalar.activation(ya[:, 0, :], res[:, t, lo:lo + 512], ACT.Square, accum_out=small[:, col:col + 1]))
                        n += 1
                    if half == 1:
                        link(nc.scalar.activation(ya[:, 1, 0:4], small[:, 160 + 4 * t:164 + 4 * t], ACT.Copy, accum_out=small[:, 180 + t:181 + t]))
                        nc.scalar.activation(small[:, 184 + t:185 + t], small[:, 180 + t:181 + t], ACT.Sqrt, bias=small[:, 250:251],
                                             scale=1.0 / D).then_inc(squares_done, 1)
                        if t:
                            scale_rest(t - 1)
            scale_rest(TOK - 1)

        @block.vector
        def _(dve):
            v = nc.vector
            count = [0]

            def link(ins):
                count[0] += 1
                ins.then_inc(v_step, 1)
                dve.wait_ge(v_step, count[0])

            def rounded(out_ap, in_ap, factor):
                link(v.tensor_scalar(out_ap, in_ap, factor, ROUND, ALU.mult, ALU.add))
                link(v.tensor_scalar(out_ap, out_ap, ROUND, None, ALU.subtract))

            def reduce_angle(r, k):
                for turns in (4096.0, 1.0):
                    rounded(k, r, INV_2PI / turns)
                    for part in split12(2.0 * np.pi * turns):
                        link(v.scalar_tensor_tensor(r, k, -part, r, ALU.mult, ALU.add))
                link(v.tensor_scalar(r, r, PI, -PI, ALU.min, ALU.max))

            def rotate(buf, table, partner, n_rows=P, col0=0):
                n_cols = buf.shape[-1]
                t = tmp[0:n_rows, 0:n_cols]
                link(v.stream_shuffle(t, buf, partner))
                link(v.tensor_tensor(t, t, table[0:n_rows, 1, col0:col0 + n_cols], ALU.mult))
                link(v.tensor_tensor(buf, buf, table[0:n_rows, 0, col0:col0 + n_cols], ALU.mult))
                return v.tensor_tensor(buf, buf, t, ALU.add)

            link(v.memset(small[:, 250:251], EPS))
            v.memset(small[:, 251:252], PI / 2).then_inc(par_go, 1)

            def low_of_h(t):
                for kq in range(4):
                    n = 4 * t + kq
                    dve.wait_ge(h_high, n + 1)
                    part = (slice(None), slice(4 * kq, 4 * kq + 4), slice(t * P, (t + 1) * P))
                    v.tensor_tensor(act_lo[part], banks[n % 8][:, :].rearrange("p (k n) -> p k n", k=4),
                                    act_hi[part].bitcast(F32), ALU.subtract).then_inc(h_low, 1)

            def norm(t):
                dve.wait_ge(rms_done, t + 1)
                v.reciprocal(small[:, 4 + t:5 + t], small[:, 8 + t:9 + t]).then_inc(rstd_ready, 1)
                dve.wait_ge(rstd_ready, t + 1)
                if t in (0, 3):
                    v.scalar_tensor_tensor(xt[:, t, :], xt[:, t, :], small[:, 4 + t:5 + t], g_row[:, :], ALU.mult, ALU.mult
                                           ).then_inc(h_ready, 1)
                else:
                    dve.wait_ge(xg_ready, t)
                    v.tensor_scalar(xt[:, t, :], xg[:, t - 1, :], small[:, 4 + t:5 + t], None, ALU.mult).then_inc(h_ready, 1)

            dve.wait_ge(g_loaded, 16)
            norm(0)
            low_of_h(0)
            norm(1)
            low_of_h(1)
            norm(2)
            norm(3)
            low_of_h(2)
            low_of_h(3)

            dve.wait_ge(consts_loaded, 32)
            link(v.tensor_copy(pos_f[:, :], pos_i[:, :]))
            for w in range(2):
                if w == 1:
                    dve.wait_ge(table_done, 2)
                link(v.tensor_scalar(ang[:, 0, :], pos_f[:, :], cols[:, 2 - 2 * w:3 - 2 * w], None, ALU.mult))
                reduce_angle(ang[:, 0, :], tmp[:, :])
                v.scalar_tensor_tensor(ang[:, 1, :], ang[:, 0, :], -1.0, ang[:, 0, :], ALU.mult, ALU.max).then_inc(ang_ready, 1)
                dve.wait_ge(ang_ready, w + 1)

            idx_partner = [q + 8 if q < 8 else q - 8 if q < 16 else q for q in range(32)]
            head_partner = [(q + 16) % 32 for q in range(32)]
            dve.wait_ge(kidx_raw, 1)
            dve.wait_ge(table_done, 2)
            link(rotate(k_raw[0:IDX_DIM, :], rot_idx, idx_partner, IDX_DIM))
            for rows in (slice(0, IDX_DIM), slice(IDX_DIM, P)):
                link(v.tensor_copy(kidx_hi[rows, :], k_raw[0:IDX_DIM, :]))
            for rows in (slice(0, IDX_DIM), slice(IDX_DIM, P)):
                v.tensor_tensor(kidx_lo[rows, :], k_raw[0:IDX_DIM, :], kidx_hi[0:IDX_DIM, :].bitcast(F32), ALU.subtract
                                ).then_inc(kidx_ready, 1)
            for i in range(8):
                dve.wait_ge(tile_free, TILE0["qidx"] + i + 1)
                raw = q_raw[:, i % 2, 0:SEQ - P]
                link(rotate(raw, rot_idx, idx_partner, P, P))
                for h in (2 * i, 2 * i + 1):
                    high = slice(IDX_DIM * (h % 2), IDX_DIM * (h % 2) + IDX_DIM)
                    low = slice(IDX_DIM - high.start, P - high.start)
                    link(v.tensor_copy(q_parts(h)[high], raw[high]))
                    last = v.tensor_tensor(q_parts(h)[low], raw[high], q_parts(h)[high].bitcast(F32), ALU.subtract)
                    if h % 2 == 0:
                        link(last)
                last.then_inc(qidx_ready, 1)
                dve.wait_ge(qidx_ready, i + 1)

            start = {1: 0, 2: 2 * P, 3: 5 * P}
            scores = {b: score[:, start[b]:start[b] + (b + 1) * P] for b in start}
            dve.wait_ge(wv_ready, 1)

            def add_item(n):
                b, h = 1 + n // IDX_HEADS, n % IDX_HEADS
                dve.wait_ge(relu_done, n + 1)
                r, w = relu[:, n % 2, 0:(b + 1) * P], w_idx[:, b, h:h + 1]
                if h == 0:
                    ins = v.tensor_scalar(scores[b], r, w, None, ALU.mult)
                else:
                    ins = v.scalar_tensor_tensor(scores[b], r, w, scores[b], ALU.mult, ALU.add)
                ins.then_inc(acc_done, 1)
                dve.wait_ge(acc_done, n + 1)

            def open_topk(b):
                link(v.memset(scores[b][0:CHUNK, (b + 1) * P - CHUNK:(b + 1) * P], MASKED))

            def topk_round(b):
                link(v.max(small[:, 12:20], scores[b]))
                link(v.match_replace(scores[b], small[:, 12:20], scores[b], REPLACED))

            def close_topk(b):
                link(v.tensor_scalar(scores[b], scores[b], TOOK_BELOW, MASKED, ALU.is_gt, ALU.mult))

            n = 0
            for b in range(1, TOK):
                for h in range(IDX_HEADS):
                    add_item(n)
                    if b > 1:
                        topk_round(b - 1)
                    n += 1
                    if n % ITEMS_PER_UNIT == 0:
                        unit = n // ITEMS_PER_UNIT - 1
                        t = TILE0["k"] + unit
                        if unit < 2 or unit >= 4:
                            dve.wait_ge(tile_free, t + 1)
                            buf = kT[:, unit, :] if unit < 2 else qT[:, unit - 4, :]
                            rotate(buf, rot_head, head_partner).then_inc(qk_ready, 1)
                            dve.wait_ge(qk_ready, unit + 1 if unit < 2 else unit - 1)
                if b > 1:
                    close_topk(b - 1)
                open_topk(b)
            for _ in range(TOPK // 8):
                topk_round(TOK - 1)
            close_topk(TOK - 1)
            link(v.memset(bias0[:, :], 0.0))
            link(v.memset(bias0[0:CHUNK, CHUNK:P], MASKED))
            biases = [bias0[:, :]] + [scores[b] for b in range(1, TOK)]

            (AR, AI, LDT, DT, ZR, MAG, KT, LBR, TH, SIN, ATH, COS, LBI, DEN, T1, T2, CR, CI) = range(18)
            RDEN, LM = LDT, DT

            def p_(i):
                return par[:, i, :]

            def tt(o_, a_, b_, op):
                link(v.tensor_tensor(o_, a_, b_, op))

            dve.wait_ge(par_done, 1)
            v.tensor_tensor(p_(ZR), p_(AR), p_(DT), ALU.mult).then_inc(par_go, 1)
            tt(p_(TH), p_(AI), p_(DT), ALU.mult)
            reduce_angle(p_(TH), p_(KT))
            v.scalar_tensor_tensor(p_(ATH), p_(TH), -1.0, p_(TH), ALU.mult, ALU.max).then_inc(par_go, 1)
            dve.wait_ge(par_done, 4)
            tt(p_(LBR), p_(MAG), p_(COS), ALU.mult)
            tt(p_(LBI), p_(MAG), p_(SIN), ALU.mult)
            tt(p_(T1), p_(AR), p_(AR), ALU.mult)
            tt(p_(T2), p_(AI), p_(AI), ALU.mult)
            tt(p_(DEN), p_(T1), p_(T2), ALU.add)
            link(v.reciprocal(p_(RDEN), p_(DEN)))
            link(v.tensor_scalar(p_(LM), p_(LBR), 1.0, None, ALU.subtract))
            tt(p_(T1), p_(LM), p_(AR), ALU.mult)
            tt(p_(T2), p_(LBI), p_(AI), ALU.mult)
            tt(p_(T1), p_(T1), p_(T2), ALU.add)
            tt(p_(CR), p_(T1), p_(RDEN), ALU.mult)
            tt(p_(T1), p_(LBI), p_(AR), ALU.mult)
            tt(p_(T2), p_(LM), p_(AI), ALU.mult)
            tt(p_(T1), p_(T1), p_(T2), ALU.subtract)
            tt(p_(CI), p_(T1), p_(RDEN), ALU.mult)

            rotors = [(p_(COS), p_(SIN))] + [(rot[:, 0, l, :], rot[:, 1, l, :]) for l in range(8)]
            for (c_, s_), (c2, s2) in zip(rotors, rotors[1:]):
                tt(p_(T1), c_, c_, ALU.mult)
                tt(p_(T2), s_, s_, ALU.mult)
                tt(c2, p_(T1), p_(T2), ALU.subtract)
                link(v.scalar_tensor_tensor(s2, c_, 2.0, s_, ALU.mult, ALU.mult))

            items = [(b, h) for b in range(TOK) for h in range(HEADS)]
            for s in range(len(items) + 3):
                if s < len(items):
                    b, h = items[s]
                    dve.wait_ge(scores_done, s + 1)
                    if s >= 3:
                        dve.wait_ge(p_turned, s - 2)
                    v.tensor_tensor_reduce(probs[:, s % 3, 0:(b + 1) * P], pair_bank[s % 2][:, 0:(b + 1) * P], biases[b], 1.0,
                                           REPLACED, ALU.add, ALU.max, small[:, 32 + s:33 + s]).then_inc(masked, 1)
                    dve.wait_ge(masked, s + 1)
                    v.tensor_scalar(small[:, 64 + s:65 + s], small[:, 32 + s:33 + s], -(HD ** -0.5), None, ALU.mult
                                    ).then_inc(nmax_ready, 1)
                if 1 <= s <= len(items):
                    i = s - 1
                    b, h = items[i]
                    dve.wait_ge(exp_done, i + 1)
                    link(v.reciprocal(small[:, 128 + i:129 + i], small[:, 96 + i:97 + i]))
                    pr = probs[:, i % 3, 0:(b + 1) * P]
                    v.tensor_scalar(pr, pr, small[:, 128 + i:129 + i], None, ALU.mult).then_inc(probs_ready, 1)
                if s >= 3:
                    i = s - 3
                    b, h = items[i]
                    dve.wait_ge(pv_done, i + 1)
                    if b == 0:
                        dve.wait_ge(tile_free, TILE0["attgate"] + h + 1)
                    ga = gate_a[:, h, b * P:(b + 1) * P]
                    v.tensor_tensor(ga, sum_bank[i % 2][:, 0:P], ga, ALU.mult).then_inc(att_ready, 1)
            for h in range(HEADS):
                dve.wait_ge(a_high, h + 1)
                v.tensor_tensor(a_lo[:, h, :], gate_a[:, h, :], a_hi[:, h, :].bitcast(F32), ALU.subtract).then_inc(a_low, 1)

            def spread(col, n_):
                return col.unsqueeze(2).to_broadcast([P, PAIRS, n_])

            dve.wait_ge(bc_loaded, 9 * 16)
            t_b = b_blk[:, 0, :, :, 0:1, :].rearrange("p q a b c -> p (q a b) c")
            for r, op in ((0, ALU.subtract), (1, ALU.add)):
                tt(b_bar[:, r, :, :], b_raw[:, r, :, :], spread(p_(CR), GCH), ALU.mult)
                tt(t_b, b_raw[:, 1 - r, :, :], spread(p_(CI), GCH), ALU.mult)
                tt(b_bar[:, r, :, :], b_bar[:, r, :, :], t_b, op)
            for r in range(2):
                for g in range(2):
                    dst = b_blk[:, r, :, :, g:g + 1, :].rearrange("p q a b c -> p (q a b) c")
                    link(v.tensor_scalar(dst, b_bar[:, r, :, :], cols[:, 4 + g:5 + g], None, ALU.mult))
            par_b = parity[:, :].unsqueeze(1).to_broadcast([P, QUADS, P])
            link(v.tensor_tensor(c_nat[:, 0, :, :], c_nat[:, 0, :, :], par_b, ALU.mult))
            v.tensor_tensor(c_nat[:, 1, :, :], c_nat[:, 1, :, :], par_b, ALU.mult).then_inc(ssm_w_ready, 1)
            dve.wait_ge(ssm_w_turned, 1)
            for r in range(2):
                link(v.tensor_copy(b_hi[:, r, :, :].rearrange("p q n -> p (q n)"), pair_bank[r][:, :]))
            link(v.memset(e_base[:, 0, :, 0:1], 1.0))
            link(v.memset(e_base[:, 1, :, 0:1], 0.0))
            for l in range(5):
                n_ = 2 ** l
                er, ei = e_base[:, 0, :, 0:n_], e_base[:, 1, :, 0:n_]
                rr, ri = spread(rotors[l][0], n_), spread(rotors[l][1], n_)
                ta, tb = b_raw[:, 0, :, 0:n_], b_raw[:, 1, :, 0:n_]
                tt(ta, er, rr, ALU.mult)
                tt(tb, ei, ri, ALU.mult)
                tt(e_base[:, 0, :, n_:2 * n_], ta, tb, ALU.subtract)
                tt(ta, er, ri, ALU.mult)
                tt(tb, ei, rr, ALU.mult)
                tt(e_base[:, 1, :, n_:2 * n_], ta, tb, ALU.add)

            def y_of_quad(q):
                dve.wait_ge(ssm_loaded, 3 * 16)
                dve.wait_ge(y_done, 4 * q + 4)
                v.scalar_tensor_tensor(uT[:, q, :], uT[:, q, :], g_cols[:, 36 + q:37 + q], sum_bank[q % 2][:, :],
                                       ALU.mult, ALU.add).then_inc(y_ready, 1)

            def mark(ins):
                count[0] += 1
                ins.then_inc(v_step, 1)
                return count[0]

            def e_start(j):
                v.tensor_copy(e_tab[:, j % 2, :, 0:E_BASE], e_base[:, :, j, :]).then_inc(e_grown, 1)

            def e_double(j, l):
                n_, rr = 2 ** l, rotors[l][0][:, j:j + 1]
                er, ei = e_tab[:, j % 2, 0, :], e_tab[:, j % 2, 1, :]
                dve.wait_ge(e_scaled, 4 * j + l - 4)
                v.scalar_tensor_tensor(er[:, n_:2 * n_], er[:, 0:n_], rr, e_prod[:, 1, 0:n_], ALU.mult, ALU.subtract)
                v.scalar_tensor_tensor(ei[:, n_:2 * n_], ei[:, 0:n_], rr, e_prod[:, 0, 0:n_], ALU.mult, ALU.add
                                       ).then_inc(e_grown, 1)

            def u_low_part(q):
                dve.wait_ge(u_high, q + 1)
                v.tensor_tensor(u_lo[:, :], uT[:, q, :], u_hi[:, :].bitcast(F32), ALU.subtract).then_inc(u_low, 1)

            dve.wait_ge(tile_done, TILE0["merge0"])
            for r in range(2):
                v.tensor_tensor(b_lo[r][:, :, :].rearrange("p q n -> p (q n)"), pair_bank[r][:, :],
                                b_hi[:, r, :, :].rearrange("p q n -> p (q n)").bitcast(F32), ALU.subtract).then_inc(b_split, 1)
            u_low_part(0)
            e_start(0)
            for l in range(5, 9):
                e_double(0, l)
            p0, p1, p2, p3 = prod[:, 0, :], prod[:, 1, :], prod2[:, 0, :], prod2[:, 1, :]
            zr, zi = z_ri[:, 0, :], z_ri[:, 1, :]
            br, bi = pair_bank[0][:, :], pair_bank[1][:, :]
            for j in range(PAIRS):
                er, ei = e_tab[:, j % 2, 0, :], e_tab[:, j % 2, 1, :]
                nxt = j + 1 < PAIRS
                dve.wait_ge(e_grown, 5 * (j + 1))
                dve.wait_ge(bu_done, j + 1)
                v.tensor_tensor(p0, br, er, ALU.mult)
                v.tensor_tensor(p1, bi, ei, ALU.mult)
                v.tensor_tensor(p2, bi, er, ALU.mult)
                v.tensor_tensor(p3, br, ei, ALU.mult).then_inc(bu_used, 1)
                if nxt:
                    e_start(j + 1)
                if nxt and j % 4 == 3:
                    u_low_part((j + 1) // 4)
                dve.wait_ge(bu_used, j + 1)
                v.tensor_tensor(zr, p0, p1, ALU.add)
                a = mark(v.tensor_tensor(zi, p2, p3, ALU.subtract))
                if nxt:
                    e_double(j + 1, 5)
                dve.wait_ge(v_step, a)
                mag = p_(MAG)[:, j:j + 1].to_broadcast([P, SEQ])
                v.tensor_tensor_scan(zr, mag, zr, 0.0, ALU.mult, ALU.add)
                a = mark(v.tensor_tensor_scan(zi, mag, zi, 0.0, ALU.mult, ALU.add))
                if nxt:
                    e_double(j + 1, 6)
                dve.wait_ge(v_step, a)
                v.tensor_tensor(p0, zr, er, ALU.mult)
                v.tensor_tensor(p1, zi, ei, ALU.mult)
                v.tensor_tensor(p2, zr, ei, ALU.mult)
                a = mark(v.tensor_tensor(p3, zi, er, ALU.mult))
                if nxt:
                    e_double(j + 1, 7)
                dve.wait_ge(v_step, a)
                if j:
                    dve.wait_ge(y_done, j)
                v.tensor_tensor(x_ri[:, 0, :], p0, p1, ALU.subtract)
                v.tensor_tensor(x_ri[:, 1, :], p2, p3, ALU.add).then_inc(x_ready, 1)
                if nxt:
                    e_double(j + 1, 8)
                if j >= 5 and j % 4 == 1:
                    y_of_quad(j // 4 - 1)
                dve.wait_ge(x_ready, j + 1)
            y_of_quad(QUADS - 1)

            def split_s(k, ready):
                link(v.tensor_copy(s_hi[:, k, :], uT[:, k, :]))
                v.tensor_tensor(s_lo[:, k, :], uT[:, k, :], s_hi[:, k, :].bitcast(F32), ALU.subtract).then_inc(ready, 1)

            for k in range(QUADS):
                dve.wait_ge(gelu_done, k + 1)
                split_s(k, s_ready)
            for n_, seg, gate_ in ((0, "ssmgate", gate_s), (1, "glu", gate_glu)):
                for k in range(QUADS):
                    dve.wait_ge(tile_free, TILE0[seg] + k + 1)
                    link(v.tensor_tensor(uT[:, k, :], uT[:, k, :], gate_[:, k, :], ALU.mult))
            for k in range(QUADS):
                split_s(k, g_ready)
            dve.wait_ge(gate_used, KD)

            def low_of_merge(k):
                m_hi, m_lo = (s_hi, s_lo) if k < QUADS else (act_hi, act_lo)
                dve.wait_ge(m_high, k + 1)
                v.tensor_tensor(m_lo[:, k, :], ya[:, k, :], m_hi[:, k, :].bitcast(F32), ALU.subtract).then_inc(m_low, 1)

            for j in range(KD):
                dve.wait_ge(tile_free, TILE0["ssmout"] + j + 1 if j < EARLY else merge1_tile(j) + 1)
                g_ = gate[:, j % 2, :]
                link(v.tensor_tensor(g_, g_, yb[:, j, :], ALU.mult))
                v.tensor_tensor(ya[:, j, :], ya[:, j, :], g_, ALU.add).then_inc(gate_used, 1)
                if 9 <= j < 9 + QUADS:
                    low_of_merge(j - 9)
            for k in range(QUADS, KD):
                low_of_merge(k)

            def finish(t):
                dve.wait_ge(squares_done, t + 1)
                v.reciprocal(small[:, 188 + t:189 + t], small[:, 184 + t:185 + t]).then_inc(scale_ready, 1)
                dve.wait_ge(scale_ready, t + 1)
                v.scalar_tensor_tensor(res[:, t, 0:V_COLS], res[:, t, 0:V_COLS], small[:, 188 + t:189 + t], g_last[:, 0:V_COLS],
                                       ALU.mult, ALU.mult).then_inc(final_done, 1)

            dve.wait_ge(res_loaded, 16 * TOK)
            dve.wait_ge(gf_loaded, 16)
            for half in range(2):
                for t in range(TOK):
                    for n in range(2):
                        if (t, n) == (TOK - 1, 1):
                            dve.wait_ge(tile_done, TILE0["out"] + 8 * half + 8)
                        else:
                            dve.wait_ge(bank_done, 7 * half + 2 * t + n + 1)
                        part = res[:, t, half * 1024 + n * 512:half * 1024 + n * 512 + 512]
                        v.tensor_tensor(part, banks[2 * t + n][:, :], part, ALU.add).then_inc(bank_taken, 1)
                    if half == 1 and t >= 1:
                        finish(t - 1)
            finish(TOK - 1)


_INS = ["x", "positions", "g_norm", "w_in", "b_merge", "a_re", "a_im", "log_dt", "ssm_b_re", "ssm_b_im", "ssm_c_re",
        "ssm_c_im", "ssm_d", "w_glu", "b_glu", "w_att_out", "w_ssm_out", "w_out", "g_final"]


def kernel(**inputs):
    from concourse import bacc
    from concourse.bass_utils import run_bass_kernel_spmd

    nc = bacc.Bacc("TRN2", target_bir_lowering=False, num_devices=1)
    arrays, args = {}, []
    given = {name: np.ascontiguousarray(inputs[name]) for name in _INS} | constants()
    for name, a in given.items():
        arrays[f"in_{name}"] = a
        args.append(nc.dram_tensor(f"in_{name}", a.shape, mybir.dt.from_np(a.dtype), kind="ExternalInput").ap())
    out = nc.dram_tensor("out_dram", (1, SEQ, D), F32, kind="ExternalOutput").ap()
    hybrid_kernel(nc, *args, out)
    r = run_bass_kernel_spmd(nc, [arrays], core_ids=[0])
    return r.results[0]["out_dram"]
```
